# Optimizing a Trainium2 kernel written in Bass

```python
import jax, jax.numpy as jnp
from jax import lax
import numpy as np
import jax
import jax.numpy as jnp

D_MODEL = 1024
BATCH = 1
SEQ = 256
DEPTH = 2

DN_HEADS = 8
DN_HEAD_DIM = 128
DN_WIDTH = DN_HEADS * DN_HEAD_DIM
DN_CONV = 4
DN_CHUNK = 64
SWA_Q_HEADS = 16
SWA_KV_HEADS = 2
SWA_HEAD_DIM = 64
SWA_GROUP = SWA_Q_HEADS // SWA_KV_HEADS
SWA_WIDTH = SWA_Q_HEADS * SWA_HEAD_DIM
SWA_KV_WIDTH = SWA_KV_HEADS * SWA_HEAD_DIM
WINDOW = 128
SWA_BLOCK = 128
ROPE_THETA = 500000.0
ROPE_DIM = SWA_HEAD_DIM // 4
D_FF = 2816
FFN_CONV = 3
EPS = 1e-6
IN_SIZES = (3 * DN_WIDTH, DN_WIDTH, DN_HEADS, DN_HEADS, SWA_WIDTH, SWA_KV_WIDTH, SWA_KV_WIDTH, D_MODEL, D_MODEL)
IN_TOTAL = 4 * DN_WIDTH + 2 * DN_HEADS + SWA_WIDTH + 2 * SWA_KV_WIDTH + 2 * D_MODEL


def _split_columns(t, sizes):
    idx, acc = [], 0
    for s in sizes[:-1]:
        acc += s
        idx.append(acc)
    return jnp.split(t, idx, axis=-1)

def rms_norm(x, w):
    xf = x.astype(jnp.float32)
    y = xf * lax.rsqrt(jnp.mean(xf * xf, axis=-1, keepdims=True) + EPS)
    return (y * w.astype(jnp.float32)).astype(x.dtype)

def l2_norm(x):
    xf = x.astype(jnp.float32)
    return (xf * lax.rsqrt(jnp.sum(xf * xf, axis=-1, keepdims=True) + EPS)).astype(x.dtype)

def causal_dwconv(x, w):
    K, C = w.shape
    return lax.conv_general_dilated(
        x, w[:, None, :].astype(x.dtype), window_strides=(1,), padding=[(K - 1, 0)],
        dimension_numbers=('NWC', 'WIO', 'NWC'), feature_group_count=C)

def partial_rope(x, pos):
    half = ROPE_DIM // 2
    inv = jnp.power(ROPE_THETA, -jnp.arange(half, dtype=jnp.float32) / half)
    ang = pos.astype(jnp.float32)[..., None] * inv
    cos, sin = jnp.cos(ang)[:, :, None, :], jnp.sin(ang)[:, :, None, :]
    xr = x[..., :ROPE_DIM].astype(jnp.float32)
    x1, x2 = xr[..., :half], xr[..., half:]
    rot = jnp.concatenate([x1 * cos - x2 * sin, x2 * cos + x1 * sin], axis=-1).astype(x.dtype)
    return jnp.concatenate([rot, x[..., ROPE_DIM:]], axis=-1)

def gated_delta_rule_chunked(q, k, v, g, beta):
    B, T, H, Dk = q.shape
    Dv = v.shape[-1]
    C = DN_CHUNK
    N = T // C
    f32 = jnp.float32

    def chunks(t):
        return t.astype(f32).reshape(B, N, C, H, -1).transpose(0, 3, 1, 2, 4)

    qc = chunks(q) * (Dk ** -0.5)
    kc, vc = chunks(k), chunks(v)
    gc = jnp.cumsum(g.astype(f32).reshape(B, N, C, H).transpose(0, 3, 1, 2), axis=-1)
    bc = beta.astype(f32).reshape(B, N, C, H).transpose(0, 3, 1, 2)
    tri_incl = jnp.tril(jnp.ones((C, C), dtype=bool))
    tri_strict = jnp.tril(jnp.ones((C, C), dtype=bool), -1)
    decay = jnp.exp(jnp.where(tri_incl, gc[..., :, None] - gc[..., None, :], -jnp.inf))
    k_beta = kc * bc[..., None]
    L = jnp.where(tri_strict, jnp.einsum('bhnid,bhnjd->bhnij', k_beta, kc) * decay, 0.0)
    A = L + jnp.eye(C, dtype=f32)
    rhs = jnp.concatenate([vc * bc[..., None], k_beta * jnp.exp(gc)[..., None]], axis=-1)
    sol = lax.linalg.triangular_solve(A, rhs, left_side=True, lower=True, unit_diagonal=True)
    u, w = sol[..., :Dv], sol[..., Dv:]
    qk = jnp.einsum('bhnid,bhnjd->bhnij', qc, kc) * decay
    q_dec = qc * jnp.exp(gc)[..., None]
    g_last = gc[..., -1]
    k_dec = kc * jnp.exp(g_last[..., None] - gc)[..., None]

    def step(S, xs):
        qd, kd, u_i, w_i, qk_i, gl = xs
        v_new = u_i - jnp.einsum('bhcd,bhde->bhce', w_i, S)
        o = jnp.einsum('bhcd,bhde->bhce', qd, S) + jnp.einsum('bhij,bhje->bhie', qk_i, v_new)
        S = S * jnp.exp(gl)[..., None, None] + jnp.einsum('bhcd,bhce->bhde', kd, v_new)
        return S, o

    xs = tuple(jnp.moveaxis(t, 2, 0) for t in (q_dec, k_dec, u, w, qk, g_last))
    S0 = jnp.zeros((B, H, Dk, Dv), f32)
    _, o = lax.scan(step, S0, xs)
    return o.transpose(1, 0, 3, 2, 4).reshape(B, T, H, Dv).astype(v.dtype)

def swa_sink_attention(q, k, v, sinks):
    B, T, Hq, D = q.shape
    nb = T // SWA_BLOCK
    f32 = jnp.float32
    qb = q.astype(f32).reshape(B, nb, SWA_BLOCK, SWA_KV_HEADS, SWA_GROUP, D)

    def band(t):
        tb = t.astype(f32).reshape(B, nb, SWA_BLOCK, SWA_KV_HEADS, D)
        prev = jnp.pad(tb, ((0, 0), (1, 0), (0, 0), (0, 0), (0, 0)))[:, :-1]
        return jnp.concatenate([prev, tb], axis=2)

    kb, vb = band(k), band(v)
    s = jnp.einsum('bnqhgd,bnkhd->bnhgqk', qb, kb) * (D ** -0.5)
    qi = jnp.arange(SWA_BLOCK)[:, None]
    kj = jnp.arange(2 * SWA_BLOCK)[None, :]
    rel = qi + SWA_BLOCK - kj
    blk = jnp.arange(nb)[:, None, None]
    mask = (rel >= 0) & (rel < WINDOW) & (blk * SWA_BLOCK + kj >= SWA_BLOCK)
    s = jnp.where(mask[None, :, None, None], s, -jnp.inf)
    sink = sinks.astype(f32).reshape(1, 1, SWA_KV_HEADS, SWA_GROUP, 1, 1)
    m = jnp.maximum(jnp.max(s, axis=-1, keepdims=True), sink)
    p = jnp.exp(s - m)
    denom = jnp.sum(p, axis=-1, keepdims=True) + jnp.exp(sink - m)
    o = jnp.einsum('bnhgqk,bnkhd->bnqhgd', p / denom, vb)
    return o.reshape(B, T, Hq * D).astype(q.dtype)

def first_inputs(seed: int = 0) -> dict:
    key = jax.random.key(seed)
    ks = jax.random.split(key, 24)
    nrm = jax.random.normal
    f32 = jnp.float32
    Lr = DEPTH
    x = nrm(ks[0], (BATCH, SEQ, D_MODEL), f32)
    c = nrm(ks[1], (BATCH, D_MODEL), f32)
    positions = (jax.random.randint(ks[2], (BATCH, 1), 0, 2048, dtype=jnp.int32)
                 + jnp.arange(SEQ, dtype=jnp.int32)[None, :])
    w_ada = nrm(ks[3], (Lr, D_MODEL, 6 * D_MODEL), f32) * D_MODEL ** -0.5
    b_ada = nrm(ks[4], (Lr, 6 * D_MODEL), f32) * 0.02
    norm_mix = 1.0 + 0.02 * nrm(ks[5], (Lr, D_MODEL), f32)
    w_in = nrm(ks[6], (Lr, D_MODEL, IN_TOTAL), f32) * D_MODEL ** -0.5
    dn_conv = nrm(ks[7], (Lr, DN_CONV, 3 * DN_WIDTH), f32) * DN_CONV ** -0.5
    dn_a_log = jnp.log(jax.random.uniform(ks[8], (Lr, DN_HEADS), f32, 1.0, 16.0))
    dt = jnp.exp(jax.random.uniform(ks[9], (Lr, DN_HEADS), f32, np.log(1e-3), np.log(1e-1)))
    dn_dt_bias = jnp.log(jnp.expm1(dt))
    dn_norm = 1.0 + 0.02 * nrm(ks[10], (Lr, DN_HEAD_DIM), f32)
    w_dn_out = nrm(ks[11], (Lr, DN_WIDTH, D_MODEL), f32) * DN_WIDTH ** -0.5
    swa_q_norm = 1.0 + 0.02 * nrm(ks[12], (Lr, SWA_HEAD_DIM), f32)
    swa_k_norm = 1.0 + 0.02 * nrm(ks[13], (Lr, SWA_HEAD_DIM), f32)
    swa_sinks = nrm(ks[14], (Lr, SWA_Q_HEADS), f32)
    w_swa_out = nrm(ks[15], (Lr, SWA_WIDTH, D_MODEL), f32) * SWA_WIDTH ** -0.5
    w_o = nrm(ks[16], (Lr, D_MODEL, D_MODEL), f32) * D_MODEL ** -0.5
    norm_ffn = 1.0 + 0.02 * nrm(ks[17], (Lr, D_MODEL), f32)
    w_up = nrm(ks[18], (Lr, D_MODEL, 2 * D_FF), f32) * D_MODEL ** -0.5
    ffn_conv = nrm(ks[19], (Lr, FFN_CONV, D_FF), f32) * FFN_CONV ** -0.5
    ffn_conv_b = nrm(ks[20], (Lr, D_FF), f32) * 0.02
    w_down = nrm(ks[21], (Lr, D_FF, D_MODEL), f32) * D_FF ** -0.5
    return {"x": x, "c": c, "positions": positions, "w_ada": w_ada, "b_ada": b_ada,
            "norm_mix": norm_mix, "w_in": w_in, "dn_conv": dn_conv, "dn_a_log": dn_a_log,
            "dn_dt_bias": dn_dt_bias, "dn_norm": dn_norm, "w_dn_out": w_dn_out,
            "swa_q_norm": swa_q_norm, "swa_k_norm": swa_k_norm, "swa_sinks": swa_sinks,
            "w_swa_out": w_swa_out, "w_o": w_o, "norm_ffn": norm_ffn, "w_up": w_up,
            "ffn_conv": ffn_conv, "ffn_conv_b": ffn_conv_b, "w_down": w_down}

def first_block(x, c, positions, w_ada, b_ada, norm_mix, w_in, dn_conv, dn_a_log, dn_dt_bias,
              dn_norm, w_dn_out, swa_q_norm, swa_k_norm, swa_sinks, w_swa_out, w_o,
              norm_ffn, w_up, ffn_conv, ffn_conv_b, w_down):
    B, T, _ = x.shape
    c_act = jax.nn.silu(c)
    for l in range(DEPTH):
        mod = c_act @ w_ada[l] + b_ada[l]
        sh1, sc1, gt1, sh2, sc2, gt2 = [m[:, None, :] for m in jnp.split(mod, 6, axis=-1)]

        h = rms_norm(x, norm_mix[l]) * (1.0 + sc1) + sh1
        proj = h @ w_in[l]
        dn_qkv, dn_z, dn_a, dn_b, sw_q, sw_k, sw_v, gate_a, gate_b = _split_columns(proj, IN_SIZES)

        dn_qkv = jax.nn.silu(causal_dwconv(dn_qkv, dn_conv[l]))
        dq, dk, dv = [t.reshape(B, T, DN_HEADS, DN_HEAD_DIM) for t in jnp.split(dn_qkv, 3, axis=-1)]
        dq, dk = l2_norm(dq), l2_norm(dk)
        g = -jnp.exp(dn_a_log[l].astype(jnp.float32)) * jax.nn.softplus(
            dn_a.astype(jnp.float32) + dn_dt_bias[l].astype(jnp.float32))
        beta = jax.nn.sigmoid(dn_b.astype(jnp.float32))
        o_dn = gated_delta_rule_chunked(dq, dk, dv, g, beta)
        o_dn = rms_norm(o_dn, dn_norm[l]) * jax.nn.silu(dn_z.reshape(B, T, DN_HEADS, DN_HEAD_DIM))
        y_a = o_dn.reshape(B, T, DN_WIDTH) @ w_dn_out[l]

        sq = partial_rope(rms_norm(sw_q.reshape(B, T, SWA_Q_HEADS, SWA_HEAD_DIM), swa_q_norm[l]), positions)
        sk = partial_rope(rms_norm(sw_k.reshape(B, T, SWA_KV_HEADS, SWA_HEAD_DIM), swa_k_norm[l]), positions)
        sv = sw_v.reshape(B, T, SWA_KV_HEADS, SWA_HEAD_DIM)
        y_b = swa_sink_attention(sq, sk, sv, swa_sinks[l]) @ w_swa_out[l]

        merged = jax.nn.sigmoid(gate_a) * y_a + jax.nn.sigmoid(gate_b) * y_b
        x = x + gt1 * (merged @ w_o[l])

        h = rms_norm(x, norm_ffn[l]) * (1.0 + sc2) + sh2
        up_act, up_lin = jnp.split(h @ w_up[l], 2, axis=-1)
        up_act = causal_dwconv(up_act, ffn_conv[l]) + ffn_conv_b[l]
        x = x + gt2 * ((jax.nn.silu(up_act) * up_lin) @ w_down[l])
    return x


ATT_HEADS = 8
ATT_HEAD_DIM = 64
ATT_WIDTH = ATT_HEADS * ATT_HEAD_DIM
IDX_HEADS = 4
IDX_DIM = 64
TOPK_MAX = 256
Q_BLOCK = 128
M_HEADS = 4
M_HEAD_DIM = 128
M_WIDTH = M_HEADS * M_HEAD_DIM
CHUNK = 128
CONV_K = 4
ROPE_THETA_2 = 10000.0
IN_SIZES_2 = (ATT_WIDTH, ATT_HEAD_DIM, ATT_HEAD_DIM, IDX_HEADS * IDX_DIM, IDX_DIM, IDX_HEADS, 2 * M_WIDTH, M_WIDTH, M_WIDTH, M_HEADS, M_HEADS)
IN_COLS = ATT_WIDTH + 2 * ATT_HEAD_DIM + IDX_HEADS * IDX_DIM + IDX_DIM + IDX_HEADS + 4 * M_WIDTH + 2 * M_HEADS


def rmsnorm(x, g):
    xf = x.astype(jnp.float32)
    y = xf * lax.rsqrt(jnp.mean(xf * xf, axis=-1, keepdims=True) + EPS) * g.astype(jnp.float32)
    return y.astype(x.dtype)

def swiglu(x, w_gate, w_up, w_down):
    return (jax.nn.silu(x @ w_gate) * (x @ w_up)) @ w_down

def rope(x, pos):
    half = x.shape[-1] // 2
    inv_freq = ROPE_THETA_2 ** (-jnp.arange(half, dtype=jnp.float32) / half)
    ang = pos.astype(jnp.float32)[:, None] * inv_freq[None, :]
    cos = jnp.cos(ang)[:, None, :]
    sin = jnp.sin(ang)[:, None, :]
    xf = x.astype(jnp.float32)
    x1, x2 = xf[..., :half], xf[..., half:]
    return jnp.concatenate([x1 * cos - x2 * sin, x2 * cos + x1 * sin], axis=-1).astype(x.dtype)

def causal_conv(x, w, b):
    y = lax.conv_general_dilated(x, w.astype(x.dtype), window_strides=(1,), padding=[(CONV_K - 1, 0)],
                                 dimension_numbers=("NWC", "WIO", "NWC"), feature_group_count=x.shape[-1])
    return y + b

def split_columns(proj):
    offsets = np.cumsum(IN_SIZES_2)[:-1].tolist()
    return jnp.split(proj, offsets, axis=-1)

def dsa_attention(q, k, v, q_idx, k_idx, w_idx):
    B, S = q.shape[0], q.shape[1]
    topk = min(TOPK_MAX, S // 4)
    nb = S // Q_BLOCK
    key_pos = jnp.arange(S, dtype=jnp.int32)

    def to_blocks(a):
        return jnp.moveaxis(a.reshape((B, nb, Q_BLOCK) + a.shape[2:]), 1, 0)

    def gather(src, idx):
        return jax.vmap(lambda sb, ib: sb[ib])(src, idx)

    def one_block(args):
        qb, qib, wb, start = args
        q_pos = start + jnp.arange(Q_BLOCK, dtype=jnp.int32)
        idx_logits = jnp.einsum("bqhd,bsd->bqhs", qib, k_idx, preferred_element_type=jnp.float32) * IDX_DIM ** -0.5
        index_score = jnp.einsum("bqhs,bqh->bqs", jax.nn.relu(idx_logits), wb.astype(jnp.float32))
        index_score = jnp.where(key_pos[None, None, :] <= q_pos[None, :, None], index_score, -jnp.inf)
        _, sel = lax.top_k(index_score, topk)
        k_sel = gather(k, sel)
        v_sel = gather(v, sel)
        logits = jnp.einsum("bqhd,bqkd->bqhk", qb, k_sel, preferred_element_type=jnp.float32) * ATT_HEAD_DIM ** -0.5
        valid = (sel <= q_pos[None, :, None])[:, :, None, :]
        p = jax.nn.softmax(jnp.where(valid, logits, -jnp.inf), axis=-1)
        return jnp.einsum("bqhk,bqkd->bqhd", p.astype(v_sel.dtype), v_sel)

    starts = jnp.arange(nb, dtype=jnp.int32) * Q_BLOCK
    out = lax.map(one_block, (to_blocks(q), to_blocks(q_idx), to_blocks(w_idx), starts))
    return jnp.moveaxis(out, 0, 1).reshape(B, S, ATT_WIDTH)

def mlstm(q, k, v, i_pre, f_pre):
    B, S, NH, d = q.shape
    nc = S // CHUNK

    def chunks(a):
        a = a.astype(jnp.float32).reshape((B, nc, CHUNK, NH) + a.shape[3:])
        return jnp.moveaxis(a, 3, 1)

    qc = chunks(q)
    kc = chunks(k) * d ** -0.5
    vc = chunks(v)
    ic = chunks(i_pre)
    b = jnp.cumsum(jax.nn.log_sigmoid(chunks(f_pre)), axis=-1)
    b_last = b[..., -1]

    a = b_last[..., None] - b + ic
    a_max = a.max(axis=-1)
    wa = jnp.exp(a - a_max[..., None])
    c_chunk = jnp.einsum("bhcl,bhcld,bhcle->bhcde", wa, kc, vc)
    n_chunk = jnp.einsum("bhcl,bhcld->bhcd", wa, kc)

    def step(carry, xs):
        C, n, m = carry
        bl, am, Cc, ncu = xs
        m_new = jnp.maximum(bl + m, am)
        s_old = jnp.exp(bl + m - m_new)
        s_new = jnp.exp(am - m_new)
        C_new = s_old[..., None, None] * C + s_new[..., None, None] * Cc
        n_new = s_old[..., None] * n + s_new[..., None] * ncu
        return (C_new, n_new, m_new), (C, n, m)

    init = (jnp.zeros((B, NH, d, d), jnp.float32), jnp.zeros((B, NH, d), jnp.float32), jnp.zeros((B, NH), jnp.float32))
    xs = (jnp.moveaxis(b_last, 2, 0), jnp.moveaxis(a_max, 2, 0), jnp.moveaxis(c_chunk, 2, 0), jnp.moveaxis(n_chunk, 2, 0))
    _, (C_prev, n_prev, m_prev) = lax.scan(step, init, xs)
    C_prev = jnp.moveaxis(C_prev, 0, 2)
    n_prev = jnp.moveaxis(n_prev, 0, 2)
    m_prev = jnp.moveaxis(m_prev, 0, 2)

    g = b + m_prev[..., None]
    causal = jnp.tril(jnp.ones((CHUNK, CHUNK), dtype=bool))
    dmat = jnp.where(causal, b[..., :, None] - b[..., None, :] + ic[..., None, :], -jnp.inf)
    m_t = jnp.maximum(g, dmat.max(axis=-1))
    w_intra = jnp.exp(dmat - m_t[..., None])
    w_inter = jnp.exp(g - m_t)
    s = jnp.einsum("bhcld,bhcsd->bhcls", qc, kc) * w_intra
    num = w_inter[..., None] * jnp.einsum("bhcld,bhcde->bhcle", qc, C_prev) + jnp.einsum("bhcls,bhcse->bhcle", s, vc)
    den = w_inter * jnp.einsum("bhcld,bhcd->bhcl", qc, n_prev) + s.sum(axis=-1)
    h = num / jnp.maximum(jnp.abs(den), jnp.exp(-m_t))[..., None]
    return jnp.moveaxis(h, 1, 3).reshape(B, S, NH, d)

def hybrid_mixer(h, pos, w_in, conv_w, conv_b, gate_b, q_norm, k_norm, m_norm, w_out):
    B, S, _ = h.shape
    q, k, v, q_idx, k_idx, w_idx, qk_m, v_m, o_m, i_pre, f_pre = split_columns(h @ w_in)
    q = rope(rmsnorm(q.reshape(B, S, ATT_HEADS, ATT_HEAD_DIM), q_norm), pos)
    k = rope(rmsnorm(k, k_norm)[:, :, None, :], pos)[:, :, 0, :]
    q_idx = rope(q_idx.reshape(B, S, IDX_HEADS, IDX_DIM), pos)
    k_idx = rope(k_idx[:, :, None, :], pos)[:, :, 0, :]
    att = dsa_attention(q, k, v, q_idx, k_idx, w_idx * IDX_HEADS ** -0.5)
    qk_m = jax.nn.silu(causal_conv(qk_m, conv_w, conv_b))
    q_m, k_m = jnp.split(qk_m, 2, axis=-1)
    shape_m = (B, S, M_HEADS, M_HEAD_DIM)
    h_m = mlstm(q_m.reshape(shape_m), k_m.reshape(shape_m), v_m.reshape(shape_m),
                i_pre + gate_b[:M_HEADS], f_pre + gate_b[M_HEADS:])
    h_m = rmsnorm(h_m, m_norm).reshape(B, S, M_WIDTH).astype(h.dtype) * jax.nn.sigmoid(o_m)
    return jnp.concatenate([att, h_m], axis=-1) @ w_out

def second_inputs(seed: int = 0) -> dict:
    key = jax.random.key(seed)
    keys = jax.random.split(key, 19)

    def nrm(k, shape, scale):
        return scale * jax.random.normal(k, shape, jnp.float32)

    mix_w = ATT_WIDTH + M_WIDTH
    return {
        "x": nrm(keys[0], (BATCH, SEQ, D_MODEL), 1.0),
        "ffn1_norm": 1.0 + nrm(keys[1], (DEPTH, D_MODEL), 0.02),
        "ffn1_w_gate": nrm(keys[2], (DEPTH, D_MODEL, D_FF), D_MODEL ** -0.5),
        "ffn1_w_up": nrm(keys[3], (DEPTH, D_MODEL, D_FF), D_MODEL ** -0.5),
        "ffn1_w_down": nrm(keys[4], (DEPTH, D_FF, D_MODEL), D_FF ** -0.5),
        "mix_norm": 1.0 + nrm(keys[5], (DEPTH, D_MODEL), 0.02),
        "w_in": nrm(keys[6], (DEPTH, D_MODEL, IN_COLS), D_MODEL ** -0.5),
        "conv_w": nrm(keys[7], (DEPTH, CONV_K, 1, 2 * M_WIDTH), CONV_K ** -0.5),
        "conv_b": nrm(keys[8], (DEPTH, 2 * M_WIDTH), 0.02),
        "gate_b": jnp.concatenate([nrm(keys[9], (DEPTH, M_HEADS), 0.1),
                                   3.0 + nrm(keys[10], (DEPTH, M_HEADS), 0.5)], axis=-1),
        "q_norm": 1.0 + nrm(keys[11], (DEPTH, ATT_HEAD_DIM), 0.02),
        "k_norm": 1.0 + nrm(keys[12], (DEPTH, ATT_HEAD_DIM), 0.02),
        "m_norm": 1.0 + nrm(keys[13], (DEPTH, M_HEADS, M_HEAD_DIM), 0.02),
        "w_out": nrm(keys[14], (DEPTH, mix_w, D_MODEL), mix_w ** -0.5),
        "ffn2_norm": 1.0 + nrm(keys[15], (DEPTH, D_MODEL), 0.02),
        "ffn2_w_gate": nrm(keys[16], (DEPTH, D_MODEL, D_FF), D_MODEL ** -0.5),
        "ffn2_w_up": nrm(keys[17], (DEPTH, D_MODEL, D_FF), D_MODEL ** -0.5),
        "ffn2_w_down": nrm(keys[18], (DEPTH, D_FF, D_MODEL), D_FF ** -0.5),
    }

def second_block(x, ffn1_norm, ffn1_w_gate, ffn1_w_up, ffn1_w_down, mix_norm, w_in, conv_w, conv_b, gate_b,
              q_norm, k_norm, m_norm, w_out, ffn2_norm, ffn2_w_gate, ffn2_w_up, ffn2_w_down):
    pos = jnp.arange(x.shape[1], dtype=jnp.int32)
    for l in range(DEPTH):
        x = x + 0.5 * swiglu(rmsnorm(x, ffn1_norm[l]), ffn1_w_gate[l], ffn1_w_up[l], ffn1_w_down[l])
        x = x + hybrid_mixer(rmsnorm(x, mix_norm[l]), pos, w_in[l], conv_w[l], conv_b[l], gate_b[l],
                             q_norm[l], k_norm[l], m_norm[l], w_out[l])
        x = x + 0.5 * swiglu(rmsnorm(x, ffn2_norm[l]), ffn2_w_gate[l], ffn2_w_up[l], ffn2_w_down[l])
    return x


def setup_inputs(seed=0):
    out = dict(first_inputs(seed))
    for name, value in second_inputs(seed + 1).items():
        if name != "x":
            out[name + "_2"] = value
    return out


def reference(
    x, c, positions, w_ada, b_ada, norm_mix, w_in, dn_conv, dn_a_log, dn_dt_bias, dn_norm,
    w_dn_out, swa_q_norm, swa_k_norm, swa_sinks, w_swa_out, w_o, norm_ffn, w_up, ffn_conv,
    ffn_conv_b, w_down, ffn1_norm_2, ffn1_w_gate_2, ffn1_w_up_2, ffn1_w_down_2, mix_norm_2,
    w_in_2, conv_w_2, conv_b_2, gate_b_2, q_norm_2, k_norm_2, m_norm_2, w_out_2, ffn2_norm_2,
    ffn2_w_gate_2, ffn2_w_up_2, ffn2_w_down_2,
):
    x = first_block(
        x, c, positions, w_ada, b_ada, norm_mix, w_in, dn_conv, dn_a_log, dn_dt_bias, dn_norm,
        w_dn_out, swa_q_norm, swa_k_norm, swa_sinks, w_swa_out, w_o, norm_ffn, w_up, ffn_conv,
        ffn_conv_b, w_down,
    )
    return second_block(
        x, ffn1_norm_2, ffn1_w_gate_2, ffn1_w_up_2, ffn1_w_down_2, mix_norm_2, w_in_2, conv_w_2,
        conv_b_2, gate_b_2, q_norm_2, k_norm_2, m_norm_2, w_out_2, ffn2_norm_2, ffn2_w_gate_2,
        ffn2_w_up_2, ffn2_w_down_2,
    )


_drawn_inputs = setup_inputs


def setup_inputs(seed=0):
    import zlib

    import numpy as np

    out = dict(_drawn_inputs(seed))
    spreads = {}
    factors = {'norm_mix': 2.865,
     'dn_norm': 3.683,
     'swa_q_norm': 8.0,
     'swa_k_norm': 8.0,
     'ffn_conv_b': 3.102,
     'ffn1_norm_2': 4.249,
     'mix_norm_2': 2.928,
     'conv_b_2': 25.696,
     'q_norm_2': 8.0,
     'k_norm_2': 8.0,
     'm_norm_2': 6.422,
     'ffn2_norm_2': 6.161}
    for name, (base, spread) in spreads.items():
        noise = np.random.default_rng([zlib.crc32(name.encode()), seed]).standard_normal(out[name].shape)
        drawn = base * np.exp(spread * noise) if base else spread * noise
        out[name] = jnp.asarray(drawn.astype(out[name].dtype))
    for name, factor in factors.items():
        out[name] = (out[name] * factor).astype(out[name].dtype)
    return out
```

```python
from contextlib import ExitStack

import numpy as np
import concourse.bass as bass
from concourse import mybir

F32 = mybir.dt.float32
I32 = mybir.dt.int32
ALU = mybir.AluOpType
ACT = mybir.ActivationFunctionType
AXX = mybir.AxisListType.X

P = 128
T = 256
D = 1024
KT = D // P
LAYERS = 2
DFF = 2816
FT = DFF // P
FP = FT // 2
EPS = 1e-6
NEG = -1e30
HD = 8
SLOT = KT * 272
NS = 3
TOPK = T // 4

C_IDENT, C_ONES, C_TRIU, C_BLK, C_PERM1, C_PERM2 = (i * P for i in range(6))
C_MU, C_ML = 6 * P, 7 * P
C_LV = 8 * P
LEVELS = 7
C_COS2 = C_LV + LEVELS * P
C_SIN2 = C_COS2 + T
C_SWA = C_SIN2 + T
C_CAUS = C_SWA + 384
C_COL = C_CAUS + 384
COL_EPS, COL_QS, COL_INV, COL_HPI, COL_ONE, COL_KS = range(6)
C_ALL = C_COL + 8


def shape_constants():
    c = np.zeros((P, C_ALL), np.float32)
    i, j = np.arange(P)[:, None], np.arange(P)[None, :]
    c[:, C_IDENT:C_IDENT + P] = i == j
    c[:, C_ONES:C_ONES + P] = 1.0
    c[:, C_TRIU:C_TRIU + P] = i <= j
    c[:, C_BLK:C_BLK + P] = (i // 64) == (j // 64)
    for at, half in ((C_PERM1, 8), (C_PERM2, 32)):
        m = np.zeros((P, P), np.float32)
        for base in (0, 64):
            for r in range(half):
                m[base + r + half, base + r] = -1.0
                m[base + r, base + r + half] = 1.0
        c[:, at:at + P] = m
    c[:, C_MU:C_MU + P] = np.where(j >= i, 0.0, NEG)
    c[:, C_ML:C_ML + P] = np.where(j <= i, 0.0, NEG)
    for s in range(LEVELS):
        w = 1 << s
        c[:, C_LV + s * P:C_LV + (s + 1) * P] = (i // (2 * w) == j // (2 * w)) & (i // w % 2 == 1) & (j // w % 2 == 0)
    inv2 = (10000.0 ** (-np.arange(32, dtype=np.float32) / np.float32(32))).astype(np.float32)
    ang = (np.arange(T, dtype=np.float32)[None, :] * inv2[np.arange(P) % 32][:, None]).astype(np.float32)
    c[:, C_COS2:C_COS2 + T] = np.cos(ang)
    c[:, C_SIN2:C_SIN2 + T] = np.sin(ang)
    c[:, C_SWA:C_SWA + P] = np.where(j <= i, 0.0, NEG)
    c[:, C_SWA + P:C_SWA + 2 * P] = np.where(j > i, 0.0, NEG)
    c[:, C_SWA + 2 * P:C_SWA + 3 * P] = np.where(j <= i, 0.0, NEG)
    c[:, C_CAUS:C_CAUS + P] = np.where(j <= i, 0.0, NEG)
    c[:, C_CAUS + 2 * P:C_CAUS + 3 * P] = np.where(j <= i, 0.0, NEG)
    inv1 = (500000.0 ** (-np.arange(8, dtype=np.float32) / np.float32(8))).astype(np.float32)
    lane = np.arange(P) % 64
    c[:, C_COL + COL_EPS] = EPS
    c[:, C_COL + COL_QS] = np.log(128.0 ** -0.5)
    c[:, C_COL + COL_INV] = np.where(lane < 16, inv1[lane % 8], 0.0)
    c[:, C_COL + COL_HPI] = np.pi / 2
    c[:, C_COL + COL_ONE] = 1.0
    return c


VA = dict(b_ada=0, norm_mix=48, norm_ffn=56, dn_norm=64, swa_q_norm=65, swa_k_norm=66)
VB = dict(dn_conv=0)
VC = dict(ffn_conv=0, ffn_conv_b=66)
VD = dict(ffn1_norm_2=0, mix_norm_2=8, ffn2_norm_2=16, conv_w_2=24, conv_b_2=56, q_norm_2=64, k_norm_2=65, m_norm_2=66)
V_ROWS = (67, 96, 88, 70)
R_ALOG, R_DTB, R_SINK, R_GB, R_ALL = 0, 16, 32, 64, 80


def schedule():
    out = []

    def ffn(kind_a, kind_b, kind_d, l):
        for i in range(FP):
            out.append((kind_a, l, i))
            out.append((kind_b, l, i))
        out.extend((kind_d, l, i) for i in range(FP))

    for l in range(LAYERS):
        out.extend(("ada", l, i) for i in range(24))
        out.append(("s1", l, 0))
        for kind, n in (("qkv", 12), ("swq", 4), ("z", 4), ("ga", 4), ("gb", 4), ("dno", 4), ("swo", 4), ("wo", 4)):
            out.extend((kind, l, i) for i in range(n))
        ffn("ua", "ul", "ud", l)
    for l in range(LAYERS):
        ffn("g1", "u1", "d1", l)
        out.append(("s2", l, 0))
        for kind, n in (("aq", 2), ("qi", 1), ("qk", 4), ("vm", 2), ("om", 2), ("out", 4)):
            out.extend((kind, l, i) for i in range(n))
        ffn("g2", "u2", "d2", l)
    return out


def build(nc, a, out):
    chunks = schedule()
    Q = {key: q for q, key in enumerate(chunks)}
    unbanked = ("ada", "ud", "d1", "d2")
    R = {key: r for r, key in enumerate(k for k in chunks if k[0] not in unbanked)}

    with ExitStack() as ctx:
        def sb(name, *shape, dt=F32):
            return ctx.enter_context(nc.sbuf_tensor(name, list(shape), dt))

        bank = [ctx.enter_context(nc.psum_tensor(f"bank{i}", [P, 512], F32)) for i in range(8)]
        L, B = bank[0:2], bank[2:8]
        LV = [b[:, :].rearrange("p (m t) -> p m t", m=2) for b in L]

        K = sb("constants", P, C_ALL)
        x = sb("x", P, KT, T)
        h = sb("h", P, KT, T)
        ring = [sb(f"ring{i}", P, SLOT) for i in range(NS)]
        vcol = sb("vcol", P, 8, P)
        heads = sb("heads", P, R_ALL)
        nea = sb("nea", P, 16)
        ccol = sb("ccol", P, KT)
        modc = sb("modc", P, 48)
        scol = sb("scol", P, 16)
        cosr = sb("cosr", P, T)
        sinr = sb("sinr", P, T)
        lnb = sb("lnb", P, T)
        rinv = sb("rinv", P, T)
        arena = sb("arena", P, 23552)
        zbuf = sb("zbuf", P, KT, T)
        ezb = sb("ezb", P, KT, T)
        gab = sb("gab", P, KT, T)
        gbb = sb("gbb", P, KT, T)
        swq = sb("swq", P, KT, T)
        kd = sb("kd", P, 2, T)
        vtok = sb("vtok", P, 2, P)
        small = sb("small", P, 512)

        def ar(at, *shape):
            n = int(np.prod(shape))
            v = arena[:, at:at + n]
            if len(shape) == 2:
                return v.rearrange("p (a b) -> p a b", a=shape[0])
            if len(shape) == 3:
                return v.rearrange("p (a b c) -> p a b c", a=shape[0], b=shape[1])
            return v

        qkv = ar(0, 24, T)
        QM, LL, LO = ar(6144, 4, 4, P), ar(8192, 4, 4, P), ar(10240, 4, 4, P)
        Y, YT, W = ar(12288, 4, 4, P), ar(14336, 4, 4, P), ar(16384, 4, 4, P)
        KX, VX, QD = ar(18432, 4, 4, P), ar(20480, 4, 4, P), ar(22528, 2, 4, P)
        U, S1, WT, oT = ar(8192, 4, 4, P), ar(14336, 2, 4, P), ar(16384, 2, 4, P), ar(10240, HD, T)
        OSQ, ORV = ar(12288, 4, 512), ar(14336, 4, 512)
        CV, EV, SV, RV = ar(12288, 2, 512), ar(13312, 2, 512), ar(14336, 2, 512), ar(15360, 2, 512)
        T1, TU, TL = ar(16384, 2, 512), ar(17408, 2, 512), ar(18432, 2, 512)
        RSQ, RRV, rtmp = ar(16384, 5, 512), ar(19456, 5, 512), ar(12288, 512)
        xin2 = ar(16384, 2, D)
        tmp = ar(0, KT, T)
        SP = ar(0, 2, 4, 384)
        PT = ar(3072, 2, 384)
        atT = ar(12288, KT, T)
        hid = ar(0, FT, T)
        FA, FB, FC = ar(5632, 2, 512), ar(6656, 2, 512), ar(7680, 2, 512)
        mrg, yb = ar(0, KT, T), ar(2048, KT, T)
        qkm = ar(0, KT, T)
        vaug = ar(2048, 2, 4, 132)
        mAR, mMR, mT = ar(4096, 2, 4, P), ar(5120, 2, 4, P), ar(6144, 2, 4, P)
        mQD, mKX, mCA = ar(7168, 4, P), ar(7680, 4, P), ar(8192, 4, 132)
        mS, mH, mX = ar(9216, 2, 4, P), ar(10240, 2, 4, P), ar(11264, 2, 4, P)
        zf = zbuf[:, :, :].rearrange("p a b -> p (a b)")
        IX, IW, IM = zf[:, 0:384], zf[:, 384:768], zf[:, 768:1152]
        IT = zf[:, 1152:1920].rearrange("p (a b) -> p a b", a=2)
        rowst = ar(0, 8, P)
        xin = ar(1024, 2, D)
        crow, hrow = ar(3072, P), ar(3200, P)
        posf, ta, tb_, tc_ = ar(3328, T), ar(3584, T), ar(3840, T), ar(4096, T)
        posi = sb("posi", 1, T, dt=I32)

        def sm(i, n=16):
            return small[:, 16 * i:16 * i + n]

        def sm2(i, heads_):
            return small[:, 16 * i:16 * i + 2 * heads_].rearrange("p (c h) -> p c h", c=2)

        def k(at, n=P):
            return K[:, at:at + n]

        def col(i):
            return K[:, C_COL + i:C_COL + i + 1]

        ident, ones = k(C_IDENT), k(C_ONES)

        def vc(tile, l, row):
            return vcol[:, VT[tile, l], row:row + 1]

        VT = {(t_, l): (3 * l + t_ if t_ < 3 else 6 + l) for t_ in range(4) for l in range(LAYERS)}

        def bcast(v, n):
            return v.unsqueeze(2).to_broadcast([P, v.shape[1], n])

        def over(v, n):
            return v.unsqueeze(1).to_broadcast([P, n, v.shape[1]])

        def sem(name):
            return ctx.enter_context(nc.semaphore(name))

        inputs_landed = sem("inputs_landed")
        output_stored = sem("output_stored")
        chunk_multiplied = sem("chunk_multiplied")
        start_transposed = sem("start_transposed")
        norm_sum = sem("norm_sum")
        head_sum_done = sem("head_sum_done")
        decay_sums = sem("decay_sums")
        prep_done = sem("prep_done")
        winv_done = sem("winv_done")
        yinv_done = sem("yinv_done")
        kv_transposed = sem("kv_transposed")
        step_done = sem("step_done")
        osum_done = sem("osum_done")
        rope_sum = sem("rope_sum")
        rope_turned = sem("rope_turned")
        scores_done = sem("scores_done")
        probs_transposed = sem("probs_transposed")
        head_weighed = sem("head_weighed")
        final_transposed = sem("final_transposed")
        index_done = sem("index_done")
        m_sums = sem("m_sums")
        m_rows = sem("m_rows")
        m_keys = sem("m_keys")
        m_scores = sem("m_scores")
        m_state = sem("m_state")
        m_nums = sem("m_nums")
        m_turned = sem("m_turned")
        vector_order = sem("vector_order")
        scalar_order = sem("scalar_order")
        pool_order = sem("pool_order")
        start_v = sem("start_v")
        squares_ready = sem("squares_ready")
        norm_unbiased = sem("norm_unbiased")
        norm_ready = sem("norm_ready")
        conv_done = sem("conv_done")
        silu_done = sem("silu_done")
        d_x = sem("d_x")
        d_glog = sem("d_glog")
        d_gcc = sem("d_gcc")
        d_coef = sem("d_coef")
        d_exponent = sem("d_exponent")
        d_rows = sem("d_rows")
        y_updated = sem("y_updated")
        kv_ready = sem("kv_ready")
        step_copied = sem("step_copied")
        rope_normed = sem("rope_normed")
        rope_added = sem("rope_added")
        rows_masked = sem("rows_masked")
        rows_max = sem("rows_max")
        probs_ready = sem("probs_ready")
        merged = sem("merged")
        hidden_ready = sem("hidden_ready")
        gate_used = sem("gate_used")
        fconv_done = sem("fconv_done")
        x_done = sem("x_done")
        m_gates = sem("m_gates")
        m_columns = sem("m_columns")
        m_masked = sem("m_masked")
        m_kx = sem("m_kx")
        m_w = sem("m_w")
        m_ca = sem("m_ca")
        m_h = sem("m_h")
        m_added = sem("m_added")
        m_pre = sem("m_pre")
        index_read = sem("index_read")
        final_copied = sem("final_copied")
        start_a = sem("start_a")
        norm_factor = sem("norm_factor")
        conv_exp = sem("conv_exp")
        head_factor = sem("head_factor")
        d_e = sem("d_e")
        d_egc = sem("d_egc")
        d_exp = sem("d_exp")
        w_copied = sem("w_copied")
        in_copied = sem("in_copied")
        out_factor = sem("out_factor")
        rope_factor = sem("rope_factor")
        exp_done = sem("exp_done")
        probs_copied = sem("probs_copied")
        pair_copied = sem("pair_copied")
        ffn_exp = sem("ffn_exp")
        m_l = sem("m_l")
        m_arc = sem("m_arc")
        m_expd = sem("m_expd")
        m_factor = sem("m_factor")
        head_squared = sem("head_squared")
        head_normed = sem("head_normed")
        offdiag_ready = sem("offdiag_ready")
        out_squared = sem("out_squared")
        out_normed = sem("out_normed")
        rope_squared = sem("rope_squared")
        w_landed = [ctx.enter_context(nc.semaphore(f"weights_landed{i}")) for i in range(NS)]
        v_chain, a_chain = vector_order, scalar_order

        xs = [("x", 0, 4)] + [(n, l, 8) for l in range(LAYERS) for n in ("wo", "ffn")] \
            + [(n, l, 4) for l in range(LAYERS) for n in ("ffn1", "out", "ffn2")]
        X0, total_x = {}, 0
        for n, l, c in xs:
            X0[n, l] = total_x
            total_x += c

        def release(key):
            kind, l, i = key
            if kind in ("s1", "s2"):
                return in_copied, INC[key]
            if kind == "qkv":
                return conv_done, 12 * l + i + 1
            if kind == "qk":
                return conv_done, 24 + 4 * l + i + 1
            if kind in ("swq", "z", "ga", "gb", "aq", "qi", "vm", "om"):
                return in_copied, INC[key]
            if kind in ("dno", "swo"):
                return merged, 8 * l + 4 * (kind == "swo") + i + 1
            if kind == "wo":
                return x_done, X0["wo", l] + 2 * i + 2
            if kind == "out":
                return x_done, X0["out", l] + i + 1
            if kind == "ua":
                return fconv_done, FP * l + i + 1
            fi = {"ul": l, "g1": 2 + 2 * l, "u1": 2 + 2 * l, "g2": 3 + 2 * l, "u2": 3 + 2 * l}[kind]
            if kind[0] == "g":
                return gate_used, FP * (fi - 2) + i + 1
            return hidden_ready, FP * fi + i + 1

        INC, n_inc = {}, 0
        for key in chunks:
            if key[0] in ("s1", "s2", "swq", "z", "ga", "gb", "aq", "qi", "vm", "om"):
                n_inc += 1
                INC[key] = n_inc
        by_turn = {r: key for key, r in R.items()}

        block = ctx.enter_context(nc.Block())

        def slot(q):
            return ring[q % NS]

        wname = dict(ua="w_up", ul="w_up", g1="ffn1_w_gate_2", u1="ffn1_w_up_2", g2="ffn2_w_gate_2", u2="ffn2_w_up_2",
                     ud="w_down", d1="ffn1_w_down_2", d2="ffn2_w_down_2", ada="w_ada", dno="w_dn_out", swo="w_swa_out",
                     wo="w_o", out="w_out_2")
        wcol = dict(qkv=0, z=3072, swq=4112, ga=5392, gb=6416, ul=DFF)
        wcol2 = dict(aq=0, qi=640, qk=964, vm=1988, om=2500)
        S1_COLS = ((0, 5136, 256), (256, 4096, 16))
        S2_COLS = ((0, 512, 64), (64, 896, 64), (128, 576, 64), (192, 960, 4), (196, 3012, 8))

        N_IN = 4 + LAYERS * (8 + 1 + 2 + 10) + 4
        landed = {}
        total = [0] * NS
        for q, (kind, _, _) in enumerate(chunks):
            total[q % NS] += 16 * (len(S1_COLS) if kind == "s1" else len(S2_COLS) if kind == "s2" else 1)
            landed[q] = total[q % NS]

        @block.sync
        def _(sp):
            n_in = [0]

            def load(dst, src):
                sp.dma_start(dst, src).then_inc(inputs_landed, 16)
                n_in[0] += 1

            load(K[:, :], a["shape_constants"])
            load(xin[:, :, :], a["x"][0].rearrange("(b p) d -> p b d", p=P))
            load(crow[0:KT, :], a["c"].rearrange("a (k p) -> (a k) p", p=P))
            load(posi[:, :], a["positions"])
            for l in range(LAYERS):
                for tile, rows in ((0, VA), (1, VB), (2, VC), (3, VD)):
                    for name, r0 in rows.items():
                        src = a[name][l]
                        if name in ("swa_q_norm", "swa_k_norm", "q_norm_2", "k_norm_2"):
                            src = src.rearrange("(a n) -> a n", a=1)
                            load(rowst[r0:r0 + 1, VT[tile, l], 0:64], src)
                            load(rowst[r0:r0 + 1, VT[tile, l], 64:128], src)
                            continue
                        if name == "conv_w_2":
                            src = src.rearrange("k a (j p) -> (k a j) p", p=P)
                        elif name == "m_norm_2":
                            pass
                        elif len(src.shape) == 2:
                            src = src.rearrange("k (j p) -> (k j) p", p=P)
                        else:
                            src = src.rearrange("(j p) -> j p", p=P)
                        load(rowst[r0:r0 + src.shape[0], VT[tile, l], :], src)
            for at, name, n in ((R_ALOG, "dn_a_log", 16), (R_DTB, "dn_dt_bias", 16), (R_SINK, "swa_sinks", 32), (R_GB, "gate_b_2", 16)):
                load(hrow[0:1, at:at + n], a[name].rearrange("(o l) n -> o (l n)", o=1))
            assert n_in[0] == N_IN, n_in

            for q, (kind, l, i) in enumerate(chunks):
                if q >= NS:
                    sp.wait_ge(chunk_multiplied, q - NS + 1)
                s = slot(q)
                if kind in ("s1", "s2"):
                    w = a["w_in" if kind == "s1" else "w_in_2"][l].rearrange("(t p) n -> p t n", p=P)
                    dst = s[:, :].rearrange("p (t n) -> p t n", t=KT)
                    for at, c0, n in (S1_COLS if kind == "s1" else S2_COLS):
                        sp.dma_start(dst[:, :, at:at + n], w[:, :, c0:c0 + n]).then_inc(w_landed[q % NS], 16)
                    continue
                if kind in ("ud", "d1", "d2"):
                    w = a[wname[kind]][l].rearrange("(t p) n -> p t n", p=P)
                    sp.dma_start(s[:, 0:2 * D].rearrange("p (t n) -> p t n", t=2), w[:, 2 * i:2 * i + 2, :]).then_inc(w_landed[q % NS], 16)
                    continue
                if kind in wcol2:
                    w, c0 = a["w_in_2"], wcol2[kind]
                elif kind in ("qkv", "z", "swq", "ga", "gb"):
                    w, c0 = a["w_in"], wcol[kind]
                else:
                    w, c0 = a[wname[kind]], wcol.get(kind, 0)
                c0 += 256 * i
                sp.dma_start(s[:, 0:2 * D].rearrange("p (t n) -> p t n", t=KT),
                             w[l].rearrange("(t p) n -> p t n", p=P)[:, :, c0:c0 + 256]).then_inc(w_landed[q % NS], 16)
            sp.wait_ge(final_copied, 4)
            sp.dma_start(out[0].rearrange("(b p) d -> p b d", p=P), xin2[:, :, :]).then_inc(output_stored, 16)
            sp.wait_ge(output_stored, 16)

        @block.tensor
        def _(pe):
            mm, tr = nc.tensor.matmul, nc.tensor.transpose
            cnt = dict(rs=0, rp=0, sc=0, pt=0, pv=0, lot=0)

            def arrive(key):
                q = Q[key]
                pe.wait_ge(w_landed[q % NS], landed[q])
                if key in R and R[key] >= 2:
                    pe.wait_ge(*release(by_turn[R[key] - 2]))
                return slot(q)[:, 0:2 * D].rearrange("p (t n) -> p t n", t=KT)

            def linear(key, rhs, norm=None):
                w = arrive(key)
                o = LV[R[key] % 2]
                for m in range(2):
                    for t in range(KT):
                        if norm is not None and m == 0:
                            pe.wait_ge(norm_ready, KT * norm + t + 1)
                        last = mm(o[:, m, :], w[:, t, m * P:(m + 1) * P], rhs[:, t, :], start=(t == 0), stop=(t == KT - 1))
                last.then_inc(chunk_multiplied, 1)

            def sum_squares(ni):
                for t in range(KT):
                    if t % 4 == 0:
                        pe.wait_ge(squares_ready, 2 * ni + t // 4 + 1)
                    last = mm(B[4][:, 0:T], ones, tmp[:, t, :], start=(t == 0), stop=(t == KT - 1))
                last.then_inc(norm_sum, 1)

            def token_major(rhs_of, dst):
                for tt in range(2):
                    for t in range(KT):
                        last = mm(dst(tt), h[:, t, tt * P:(tt + 1) * P], rhs_of(t), start=(t == 0), stop=(t == KT - 1))
                return last

            def special(kind, l, ni):
                key = (kind, l, 0)
                arrive(key)
                w = slot(Q[key])[:, :].rearrange("p (t n) -> p t n", t=KT)
                o = LV[R[key] % 2]
                pe.wait_ge(norm_ready, KT * ni + KT)
                for m in range(2):
                    for half in range(2):
                        for t in range(KT):
                            mm(o[64 * half:64 * half + 64, m, :], w[:, t, 64 * m:64 * m + 64], h[:, t, :],
                               start=(t == 0), stop=(t == KT - 1))
                n = 144 if kind == "s1" else 76
                token_major(lambda t: w[:, t, 128:128 + n], lambda tt: B[5][:, tt * T:tt * T + n]).then_inc(chunk_multiplied, 1)

            def rope(src, normed, perm):
                for j, yes in enumerate(normed):
                    if yes:
                        n = cnt["rs"]
                        pe.wait_ge(rope_squared, n + 1)
                        if n >= 2:
                            pe.wait_ge(rope_factor, n - 1)
                        mm(B[n % 2][:, :], k(C_BLK), RSQ[:, j, :], start=True, stop=True).then_inc(rope_sum, 1)
                        cnt["rs"] += 1
                n0 = cnt["rs"] - sum(normed)
                for j, yes in enumerate(normed):
                    if yes:
                        n0 += 1
                        pe.wait_ge(rope_normed, n0)
                    n = cnt["rp"]
                    if n >= 2:
                        pe.wait_ge(rope_added, n - 1)
                    mm(B[2 + n % 2][:, :], k(perm), src[j], start=True, stop=True).then_inc(rope_turned, 1)
                    cnt["rp"] += 1

            def attention(nh, qt, g_of, v_of):
                def scores(lot):
                    for h4 in range(4):
                        hh, n = 4 * lot + h4, cnt["sc"]
                        if n >= 3:
                            pe.wait_ge(rows_masked, n - 2)
                        b, lo = B[n % 3], 64 * (hh % 2)
                        kk = kd[lo:lo + 64, g_of(hh), :]
                        mm(b[:, 0:P], qt[lo:lo + 64, hh // 2, 0:P], kk[:, 0:P], start=True, stop=True)
                        mm(b[:, P:3 * P], qt[lo:lo + 64, hh // 2, P:T], kk, start=True, stop=True).then_inc(scores_done, 1)
                        cnt["sc"] += 1

                def turn(buf, h4):
                    n = cnt["pt"]
                    if n >= 2:
                        pe.wait_ge(probs_copied, n - 1)
                    for s in range(3):
                        last = tr(B[3 + n % 2][:, s * P:(s + 1) * P], SP[:, buf, h4, s * P:(s + 1) * P], ident)
                    last.then_inc(probs_transposed, 1)
                    cnt["pt"] += 1

                def weigh(hh, n):
                    pe.wait_ge(probs_copied, n + 1)
                    pair = cnt["pv"] // 2
                    if hh % 2 == 0 and pair >= 2:
                        pe.wait_ge(pair_copied, pair - 1)
                    o = L[pair % 2][64 * (hh % 2):64 * (hh % 2) + 64, 0:T]
                    pp = PT[:, n % 2, :]
                    mm(o[:, 0:P], v_of(hh, 0), pp[:, 0:P], start=True, stop=True)
                    mm(o[:, P:T], v_of(hh, 0), pp[:, P:2 * P], start=True, stop=False)
                    mm(o[:, P:T], v_of(hh, 1), pp[:, 2 * P:3 * P], start=False, stop=True).then_inc(head_weighed, 1)
                    cnt["pv"] += 1

                scores(0)
                for lot in range(nh // 4):
                    if lot + 1 < nh // 4:
                        scores(lot + 1)
                    pe.wait_ge(probs_ready, cnt["lot"] + 1)
                    n0 = cnt["pt"]
                    turn(cnt["lot"] % 2, 0)
                    for h4 in range(4):
                        if h4 < 3:
                            turn(cnt["lot"] % 2, h4 + 1)
                        weigh(4 * lot + h4, n0 + h4)
                    cnt["lot"] += 1

            def ffn(ka, kb, kc, l, ni, fi):
                for i in range(FP):
                    linear((ka, l, i), h, norm=ni if i == 0 else None)
                    linear((kb, l, i), h)
                for i in range(FP):
                    q = Q[kc, l, i]
                    pe.wait_ge(w_landed[q % NS], landed[q])
                    pe.wait_ge(hidden_ready, FP * fi + i + 1)
                    w = slot(q)[:, 0:2 * D].rearrange("p (t n) -> p t n", t=2)
                    for t in range(2):
                        for m in range(KT):
                            last = mm(B[m // 2][:, (m % 2) * T:(m % 2) * T + T], w[:, t, m * P:(m + 1) * P], hid[:, 2 * i + t, :],
                                      start=(i == 0 and t == 0 and m % 2 == 0), stop=(i == FP - 1 and t == 1),
                                      skip_group_check=True)
                    last.then_inc(chunk_multiplied, 1)

            pe.wait_ge(inputs_landed, 16 * N_IN)
            for v in range(8):
                n = V_ROWS[v % 3] if v < 6 else V_ROWS[3]
                tr(B[v // 4][:, (v % 4) * P:(v % 4) * P + n], rowst[0:n, v, :], ident[0:n, 0:n])
            tr(B[2][:, 0:KT], crow[0:KT, :], ident[0:KT, 0:KT])
            mm(B[2][:, P:P + R_ALL], ones[0:1, :], hrow[0:1, 0:R_ALL], start=True, stop=True)
            pe.wait_ge(start_v, 1)
            mm(B[2][:, T:2 * T], ones[0:1, :], posf[0:1, :], start=True, stop=True).then_inc(start_transposed, 1)
            for u, b in enumerate((B[3], B[4], B[5], L[0])):
                for m in range(2):
                    for tt in range(2):
                        last = tr(b[:, m * T + tt * P:m * T + (tt + 1) * P], xin[:, tt, (2 * u + m) * P:(2 * u + m + 1) * P], ident)
                last.then_inc(start_transposed, 1)

            for l in range(LAYERS):
                sum_squares(2 * l)
                if l == 0:
                    pe.wait_ge(start_v, 4)
                for i in range(24):
                    w = arrive(("ada", l, i))
                    for m in range(2):
                        for t in range(KT):
                            last = mm(B[5][:, 2 * i + m:2 * i + m + 1], w[:, t, m * P:(m + 1) * P], ccol[:, t:t + 1],
                                      start=(t == 0), stop=(t == KT - 1))
                    last.then_inc(chunk_multiplied, 1)
                special("s1", l, 2 * l)
                for i in range(12):
                    linear(("qkv", l, i), h)
                    if 3 <= i < 11:
                        n = 8 * l + i - 3
                        pe.wait_ge(head_squared, n + 1)
                        if n >= 2:
                            pe.wait_ge(head_factor, n - 1)
                        mm(B[(i - 3) % 2][:, :], ones, SV[:, (i - 3) % 2, :], start=True, stop=True).then_inc(head_sum_done, 1)
                for kind in ("swq", "z", "ga", "gb"):
                    for i in range(4):
                        linear((kind, l, i), h)
                pe.wait_ge(d_glog, l + 1)
                glog = sm2(0, 8)
                mm(B[5][:, 0:16], k(C_TRIU), sm(0), start=True, stop=True).then_inc(decay_sums, 1)
                rope([swq[:, 2 * j:2 * j + 2, :] for j in range(4)] + [kd[:, :, :]], [True] * 5, C_PERM1)
                pe.wait_ge(rope_added, cnt["rp"])
                pe.wait_ge(head_normed, 8 * l + 8)
                pe.wait_ge(silu_done, 12 * l + 12)
                pe.wait_ge(d_coef, l + 1)
                for g in range(4):
                    c, h0, b = g // 2, 4 * (g % 2), 3 * (g % 2)
                    tk = slice(c * P, c * P + P)
                    if g >= 2:
                        pe.wait_ge(d_rows, 4 * l + g - 1)
                    for j in range(4):
                        mm(B[b][:, j * P:(j + 1) * P], glog[:, c, h0 + j:h0 + j + 1].to_broadcast([P, P]), k(C_TRIU), start=True, stop=True)
                    for j in range(4):
                        mm(B[b + 1][:, j * P:(j + 1) * P], qkv[:, 8 + h0 + j, tk], qkv[:, h0 + j, tk], start=True, stop=True)
                    for j in range(4):
                        last = mm(B[b + 2][:, j * P:(j + 1) * P], qkv[:, 8 + h0 + j, tk], qkv[:, 8 + h0 + j, tk], start=True, stop=True)
                    last.then_inc(prep_done, 1)
                for s in range(LEVELS):
                    for g in range(4):
                        n = 4 * (LEVELS * l + s) + g
                        wn = 4 * ((LEVELS - 1) * l + s - 1) + g
                        pe.wait_ge(offdiag_ready, n + 1)
                        if s == 0 and g >= 2:
                            pe.wait_ge(y_updated, n - 1)
                        if s == 0 and g < 2:
                            pe.wait_ge(d_rows, 4 * l + 4)
                        if s == 1:
                            pe.wait_ge(y_updated, 4 * (LEVELS * l + 1))
                        if s > 1:
                            pe.wait_ge(y_updated, n - 3)
                        if s > 1 or (s == 1 and g >= 2):
                            pe.wait_ge(w_copied, wn - 1)
                        for j in range(4):
                            last = mm(B[g % 2][:, j * P:(j + 1) * P], LO[:, g, j, :], ident if s == 0 else Y[:, g, j, :], start=True, stop=True)
                        last.then_inc(winv_done, 1)
                    for g in range(4):
                        if s == 0:
                            continue
                        n = 4 * (LEVELS * l + s) + g
                        wn = 4 * ((LEVELS - 1) * l + s - 1) + g
                        pe.wait_ge(w_copied, wn + 1)
                        if s > 1 or g >= 2:
                            pe.wait_ge(y_updated, n - 1)
                        by, bt = B[2 + 2 * (g % 2)], B[3 + 2 * (g % 2)]
                        for j in range(4):
                            last = mm(by[:, j * P:(j + 1) * P], YT[:, g, j, :], W[:, g, j, :], start=True, stop=True)
                        if s < LEVELS - 1:
                            for j in range(4):
                                last = mm(bt[:, j * P:(j + 1) * P], W[:, g, j, :], YT[:, g, j, :], start=True, stop=True)
                        last.then_inc(yinv_done, 1)
                pe.wait_ge(y_updated, 4 * LEVELS * (l + 1))
                for g in range(4):
                    c, h0 = g // 2, 4 * (g % 2)
                    tk = slice(c * P, c * P + P)
                    if g >= 2:
                        pe.wait_ge(kv_ready, 4 * l + g - 1)
                    for j in range(4):
                        tr(B[2 * (g % 2)][:, j * P:(j + 1) * P], qkv[:, 8 + h0 + j, tk], ident)
                    for j in range(4):
                        last = tr(B[2 * (g % 2) + 1][:, j * P:(j + 1) * P], qkv[:, 16 + h0 + j, tk], ident)
                    last.then_inc(kv_transposed, 1)
                pe.wait_ge(kv_ready, 4 * l + 4)
                base = 12 * l
                for hh in range(2):
                    for j in range(4):
                        last = mm(B[hh][:, j * P:(j + 1) * P], Y[:, hh, j, :], VX[:, hh, j, :], start=True, stop=True)
                    last.then_inc(step_done, 1)
                for hh in range(2):
                    for j in range(4):
                        last = mm(B[2 + hh][:, j * P:(j + 1) * P], KX[:, 2 + hh, j, :], Y[:, 2 + hh, j, :], start=True, stop=True)
                    last.then_inc(step_done, 1)
                for hh in range(2):
                    pe.wait_ge(step_copied, base + hh + 1)
                    for j in range(4):
                        last = mm(B[4 + hh][:, j * P:(j + 1) * P], KX[:, hh, j, :], U[:, hh, j, :], start=True, stop=True)
                    last.then_inc(step_done, 1)
                for hh in range(2):
                    for j in range(4):
                        last = mm(B[hh][:, j * P:(j + 1) * P], U[:, hh, j, :], QM[:, hh, j, :], start=True, stop=True)
                    last.then_inc(step_done, 1)
                for hh in range(2):
                    pe.wait_ge(step_copied, base + 5 + hh)
                    for j in range(4):
                        mm(B[2 + hh][:, j * P:(j + 1) * P], Y[:, 2 + hh, j, :], VX[:, 2 + hh, j, :], start=True, stop=False)
                        last = mm(B[2 + hh][:, j * P:(j + 1) * P], WT[:, hh, j, :], S1[:, hh, j, :], start=False, stop=True)
                    last.then_inc(step_done, 1)
                for hh in range(2):
                    pe.wait_ge(step_copied, base + 9 + hh)
                    for j in range(4):
                        mm(B[4 + hh][:, j * P:(j + 1) * P], S1[:, hh, j, :], QD[:, hh, j, :], start=True, stop=False)
                        last = mm(B[4 + hh][:, j * P:(j + 1) * P], U[:, 2 + hh, j, :], QM[:, 2 + hh, j, :], start=False, stop=True)
                    last.then_inc(step_done, 1)
                for i in range(4):
                    pe.wait_ge(out_squared, 4 * l + i + 1)
                    if i >= 2:
                        pe.wait_ge(out_factor, 4 * l + i - 1)
                    mm(B[i % 2][:, :], ones, OSQ[:, i, :], start=True, stop=True).then_inc(osum_done, 1)
                pe.wait_ge(out_factor, 4 * l + 4)
                pe.wait_ge(in_copied, INC["gb", l, 3])
                attention(16, swq, lambda hh: hh // 8, lambda hh, tt: vtok[:, tt, 64 * (hh // 8):64 * (hh // 8) + 64])
                pe.wait_ge(out_normed, l + 1)
                pe.wait_ge(pair_copied, cnt["pv"] // 2)
                for i in range(4):
                    linear(("dno", l, i), oT)
                pe.wait_ge(pair_copied, cnt["pv"] // 2)
                for i in range(4):
                    linear(("swo", l, i), atT)
                pe.wait_ge(merged, 8 * l + 8)
                for i in range(4):
                    linear(("wo", l, i), mrg)
                sum_squares(2 * l + 1)
                ffn("ua", "ul", "ud", l, 2 * l + 1, l)

            for l in range(LAYERS):
                ni = 4 + 3 * l
                sum_squares(ni)
                ffn("g1", "u1", "d1", l, ni, 2 + 2 * l)
                sum_squares(ni + 1)
                special("s2", l, ni + 1)
                for kind, n in (("aq", 2), ("qi", 1), ("qk", 4)):
                    for i in range(n):
                        linear((kind, l, i), h)
                for i in range(2):
                    w = arrive(("vm", l, i))
                    o = LV[R["vm", l, i] % 2]
                    token_major(lambda t: w[:, t, :], lambda tt: o[:, tt, :]).then_inc(chunk_multiplied, 1)
                for i in range(2):
                    linear(("om", l, i), h)
                rope([swq[:, 0:2, :], swq[:, 2:4, :], swq[:, 4:6, :], kd[:, :, :]], [True, True, False, True], C_PERM2)
                pe.wait_ge(rope_added, cnt["rp"])
                for hh in range(4):
                    if hh >= 2:
                        pe.wait_ge(index_read, 4 * l + hh - 1)
                    b, lo = B[hh % 2], 64 * (hh % 2)
                    kk = kd[lo:lo + 64, 1, :]
                    mm(b[:, 0:P], swq[lo:lo + 64, 4 + hh // 2, 0:P], kk[:, 0:P], start=True, stop=True)
                    mm(b[:, P:3 * P], swq[lo:lo + 64, 4 + hh // 2, P:T], kk, start=True, stop=True).then_inc(index_done, 1)
                pe.wait_ge(m_gates, l + 1)
                nlf, gi = sm2(0, 4), sm2(1, 4)
                mm(B[2][:, 0:8], k(C_TRIU), sm(0, 8), start=True, stop=True)
                mm(B[2][:, 8:16], ones, sm(0, 8), start=True, stop=True).then_inc(m_sums, 1)
                for c in range(2):
                    for j in range(4):
                        o = B[3 + c][:, j * P:(j + 1) * P]
                        mm(o, gi[:, c, j:j + 1].to_broadcast([P, P]), ident, start=True, stop=False)
                        last = mm(o, nlf[:, c, j:j + 1].to_broadcast([P, P]), k(C_TRIU), start=False, stop=True)
                last.then_inc(m_rows, 1)
                pe.wait_ge(silu_done, 24 + 4 * l + 4)
                for j in range(4):
                    last = tr(B[5][:, j * P:(j + 1) * P], qkm[:, 4 + j, 0:P], ident)
                last.then_inc(m_keys, 1)
                pe.wait_ge(m_arc, l + 1)
                for c in range(2):
                    for j in range(4):
                        last = mm(B[3 + c][:, j * P:(j + 1) * P], qkm[:, 4 + j, c * P:(c + 1) * P], qkm[:, j, c * P:(c + 1) * P], start=True, stop=True)
                last.then_inc(m_scores, 1)
                pe.wait_ge(m_kx, l + 1)
                pe.wait_ge(m_columns, l + 1)
                pe.wait_ge(in_copied, INC["vm", l, 1])
                for j in range(4):
                    last = mm(B[2 if j < 2 else 5][:, (j % 2) * T:(j % 2) * T + 129], mKX[:, j, :], vaug[:, 0, j, 0:129], start=True, stop=True)
                last.then_inc(m_state, 1)
                pe.wait_ge(m_ca, l + 1)
                pe.wait_ge(index_read, 4 * l + 4)
                for c in range(2):
                    for j in range(4):
                        o = B[(3, 4, 0, 1)[2 * c + j // 2]][:, (j % 2) * T:(j % 2) * T + 129]
                        last = mm(o, mS[:, c, j, :], vaug[:, c, j, 0:129], start=True, stop=(c == 0))
                        if c == 1:
                            last = mm(o, mQD[:, j, :], mCA[:, j, 0:129], start=False, stop=True)
                last.then_inc(m_nums, 1)
                pe.wait_ge(m_h, l + 1)
                for c in range(2):
                    for j in range(4):
                        last = tr(B[2 if c == 0 else 5][:, j * P:(j + 1) * P], mH[:, c, j, :], ident)
                last.then_inc(m_turned, 1)
                pe.wait_ge(m_added, l + 1)
                pe.wait_ge(in_copied, INC["om", l, 1])
                attention(8, swq, lambda hh: 0, lambda hh, tt: vtok[:, tt, 0:64])
                pe.wait_ge(pair_copied, cnt["pv"] // 2)
                for i in range(4):
                    linear(("out", l, i), atT)
                sum_squares(ni + 2)
                ffn("g2", "u2", "d2", l, ni + 2, 3 + 2 * l)
            pe.wait_ge(x_done, total_x)
            for u in range(4):
                for j in range(4):
                    last = tr(B[u][:, j * P:(j + 1) * P], x[:, 4 * (u % 2) + j, (u // 2) * P:(u // 2) * P + P], ident)
                last.then_inc(final_transposed, 1)
        @block.vector
        def _(dve):
            v = nc.vector
            count = [0]

            def then(*ins):
                for i in ins:
                    i.then_inc(v_chain, 1)
                count[0] += len(ins)
                dve.wait_ge(v_chain, count[0])

            B5v = B[5][:, :].rearrange("p (c n) -> p c n", c=2)

            def square(ni, x_count):
                dve.wait_ge(x_done, x_count)
                for s in range(2):
                    xx = x[:, 4 * s:4 * s + 4, :]
                    v.tensor_tensor(tmp[:, 4 * s:4 * s + 4, :], xx, xx, ALU.mult).then_inc(squares_ready, 1)

            def scale(ni, cols, biased):
                dve.wait_ge(norm_factor, ni + 1)
                for t in range(KT):
                    v.scalar_tensor_tensor(out=(tmp if biased else h)[:, t, :], in0=x[:, t, :], scalar=cols(t), in1=rinv[:, :],
                                               op0=ALU.mult, op1=ALU.mult).then_inc(norm_unbiased if biased else norm_ready, 1)

            def conv(key, n, taps, cols, bias):
                dve.wait_ge(chunk_multiplied, Q[key] + 1)
                if n >= 2:
                    dve.wait_ge(silu_done, n - 1)
                ps = LV[R[key] % 2]
                dst = CV[:, n % 2, :].rearrange("p (m t) -> p m t", m=2)
                causal_taps(ps, dst, taps, cols, bias, conv_done)

            def causal_taps(ps, dst, taps, cols, bias, signal):
                then(*[v.tensor_scalar(dst[:, m, :], ps[:, m, :], cols(taps - 1, m), bias(m) if bias else None,
                                       ALU.mult, ALU.add) if bias else
                       v.tensor_scalar(dst[:, m, :], ps[:, m, :], cols(taps - 1, m), None, ALU.mult) for m in range(2)])
                for s in range(1, taps):
                    ins = [v.scalar_tensor_tensor(out=dst[:, m, s:T], in0=ps[:, m, 0:T - s], scalar=cols(taps - 1 - s, m),
                                                  in1=dst[:, m, s:T], op0=ALU.mult, op1=ALU.add) for m in range(2)]
                    if s < taps - 1:
                        then(*ins)
                    else:
                        then(ins[0])
                        ins[1].then_inc(signal, 1)

            def silu(n, dst):
                dve.wait_ge(conv_exp, n + 1)
                e = EV[:, n % 2, :]
                then(v.tensor_scalar_add(e, e, 1.0))
                then(v.reciprocal(e, e))
                v.tensor_tensor(dst, CV[:, n % 2, :].rearrange("p (m t) -> p m t", m=2), e.rearrange("p (m t) -> p m t", m=2),
                                    ALU.mult).then_inc(silu_done, 1)

            def sigmoid(buf):
                then(v.tensor_scalar_add(buf, buf, 1.0))
                then(v.reciprocal(buf, buf))

            turned, factored, normed_n = [0], [0], [0]

            def rope(pieces, cos, sin):
                for j, (src, w, tiles) in enumerate(pieces):
                    if w is None:
                        continue
                    factored[0] += 1
                    dve.wait_ge(rope_factor, factored[0])
                    r = RRV[:, j, :].rearrange("p (m t) -> p m t", m=2)
                    v.scalar_tensor_tensor(out=src[:, 0:tiles, :], in0=src[:, 0:tiles, :], scalar=w, in1=r[:, 0:tiles, :],
                                               op0=ALU.mult, op1=ALU.mult).then_inc(rope_normed, 1)
                dve.wait_ge(rope_normed, factored[0])
                rt = rtmp.rearrange("p (m t) -> p m t", m=2)
                for src, _, _ in pieces:
                    n = turned[0]
                    dve.wait_ge(rope_turned, n + 1)
                    if n:
                        dve.wait_ge(rope_added, n)
                    then(v.tensor_tensor(rt, B[2 + n % 2][:, :].rearrange("p (m t) -> p m t", m=2), over(sin, 2), ALU.mult),
                         v.tensor_tensor(src, src, over(cos, 2), ALU.mult))
                    v.tensor_tensor(src, src, rt, ALU.add).then_inc(rope_added, 1)
                    turned[0] += 1

            scored, lots = [0], [0]

            def attention(nh, mask, sink):
                def masked(lot):
                    gl = lots[0] + lot
                    buf = gl % 2
                    if gl >= 2:
                        dve.wait_ge(probs_transposed, 4 * (gl - 1))
                    for h4 in range(4):
                        n = scored[0]
                        dve.wait_ge(scores_done, n + 1)
                        v.scalar_tensor_tensor(out=SP[:, buf, h4, :], in0=B[n % 3][:, 0:384], scalar=0.125, in1=mask,
                                                   op0=ALU.mult, op1=ALU.add).then_inc(rows_masked, 1)
                        scored[0] += 1
                    dve.wait_ge(rows_masked, scored[0])
                    nm = sm2(10 + buf, 4)
                    then(v.tensor_reduce(nm[:, 0, :], SP[:, buf, :, 0:P], AXX, ALU.max),
                         v.tensor_reduce(nm[:, 1, :], SP[:, buf, :, P:3 * P], AXX, ALU.max))
                    if sink is not None:
                        sk = over(sink[:, 4 * lot:4 * lot + 4], 2)
                        then(v.tensor_tensor(nm, nm, sk, ALU.max))
                    last = v.tensor_scalar(nm, nm, -1.0, None, ALU.mult)
                    if sink is not None:
                        then(last)
                        last = v.tensor_tensor(sm2(14 + buf, 4), nm, sk, ALU.add)
                    last.then_inc(rows_max, 1)

                def normalised(lot):
                    gl = lots[0] + lot
                    buf = gl % 2
                    dve.wait_ge(exp_done, gl + 1)
                    rs = sm(12 + buf, 8)
                    if sink is not None:
                        then(v.tensor_tensor(rs, rs, sm(14 + buf, 8), ALU.add))
                    then(v.reciprocal(rs, rs))
                    r = sm2(12 + buf, 4)
                    then(v.tensor_tensor(SP[:, buf, :, 0:P], SP[:, buf, :, 0:P], bcast(r[:, 0, :], P), ALU.mult))
                    v.tensor_tensor(SP[:, buf, :, P:3 * P], SP[:, buf, :, P:3 * P], bcast(r[:, 1, :], 2 * P), ALU.mult).then_inc(probs_ready, 1)

                n = nh // 4
                masked(0)
                for lot in range(n):
                    if lot + 1 < n:
                        masked(lot + 1)
                    normalised(lot)
                lots[0] += n

            def hidden(key, fi, i, act):
                dve.wait_ge(chunk_multiplied, Q[key] + 1)
                v.tensor_tensor(hid[:, 2 * i:2 * i + 2, :], act.rearrange("p (m t) -> p m t", m=2), LV[R[key] % 2], ALU.mult).then_inc(hidden_ready, 1)

            def gated_ffn(ka, kb, kc, l, fi, name):
                for i in range(FP):
                    dve.wait_ge(ffn_exp, FP * fi + i + 1)
                    if i >= 2:
                        dve.wait_ge(hidden_ready, FP * fi + i - 1)
                    fa = FA[:, i % 2, :]
                    sigmoid(fa)
                    v.tensor_tensor(FB[:, i % 2, :], fa, L[R[ka, l, i] % 2][:, :], ALU.mult).then_inc(gate_used, 1)
                    dve.wait_ge(gate_used, FP * (fi - 2) + i + 1)
                    hidden((kb, l, i), fi, i, FB[:, i % 2, :])
                dve.wait_ge(chunk_multiplied, Q[kc, l, FP - 1] + 1)
                for m in range(4):
                    xx = x[:, 2 * m:2 * m + 2, :]
                    v.scalar_tensor_tensor(out=xx, in0=B[m][:, :].rearrange("p (m t) -> p m t", m=2), scalar=0.5, in1=xx,
                                               op0=ALU.mult, op1=ALU.add).then_inc(x_done, 1)

            dve.wait_ge(inputs_landed, 16 * N_IN)
            v.tensor_copy(posf[0:1, :], posi[:, :]).then_inc(start_v, 1)
            dve.wait_ge(start_transposed, 1)
            ins = []
            for n in range(8):
                r = V_ROWS[n % 3] if n < 6 else V_ROWS[3]
                ins.append(v.tensor_copy(vcol[:, n, 0:r], B[n // 4][:, (n % 4) * P:(n % 4) * P + r]))
            ins.append(v.tensor_copy(ccol[:, :], B[2][:, 0:KT]))
            ins.append(v.tensor_copy(heads[:, :], B[2][:, P:P + R_ALL]))
            ins.append(v.tensor_scalar(ta, B[2][:, T:2 * T], col(COL_INV), None, ALU.mult))
            then(*ins)
            v.tensor_scalar(tb_, ta, float(1 / (2 * np.pi)), 12582912.0, ALU.mult, ALU.add).then_inc(start_v, 1)
            dve.wait_ge(start_v, 2)
            then(v.tensor_scalar(tb_, tb_, 12582912.0, None, ALU.subtract))
            then(v.scalar_tensor_tensor(out=ta, in0=tb_, scalar=-6.28125, in1=ta, op0=ALU.mult, op1=ALU.add))
            then(v.scalar_tensor_tensor(out=ta, in0=tb_, scalar=-(2 * np.pi - 6.28125), in1=ta, op0=ALU.mult, op1=ALU.add))
            then(v.tensor_scalar(ta, ta, 3.1415925, -3.1415925, ALU.min, ALU.max))
            v.scalar_tensor_tensor(out=tc_, in0=ta, scalar=-1.0, in1=ta, op0=ALU.mult, op1=ALU.max).then_inc(start_v, 1)
            for u, b in enumerate((B[3], B[4], B[5], L[0])):
                dve.wait_ge(start_transposed, u + 2)
                v.tensor_copy(x[:, 2 * u:2 * u + 2, :], b[:, :].rearrange("p (m t) -> p m t", m=2)).then_inc(x_done, 1)
            dve.wait_ge(start_a, 1)
            then(v.tensor_scalar_add(modc[:, 0:KT], modc[:, 0:KT], 1.0), v.tensor_scalar(nea[:, :], nea[:, :], -1.0, None, ALU.mult))
            then(v.reciprocal(modc[:, 0:KT], modc[:, 0:KT]))
            v.tensor_tensor(ccol[:, :], ccol[:, :], modc[:, 0:KT], ALU.mult).then_inc(start_v, 1)
            dve.wait_ge(start_v, 4)

            for l in range(LAYERS):
                va = VT[0, l]
                square(2 * l, X0["wo", l])
                dve.wait_ge(chunk_multiplied, Q["ada", l, 23] + 1)
                then(v.tensor_tensor(modc[:, :], B[5][:, 0:48], vcol[:, va, 0:48], ALU.add))
                then(v.scalar_tensor_tensor(out=scol[:, 0:8], in0=modc[:, 8:16], scalar=1.0, in1=vcol[:, va, 48:56], op0=ALU.add, op1=ALU.mult),
                     v.scalar_tensor_tensor(out=scol[:, 8:16], in0=modc[:, 32:40], scalar=1.0, in1=vcol[:, va, 56:64], op0=ALU.add, op1=ALU.mult))
                scale(2 * l, lambda t: scol[:, t:t + 1], True)
                dve.wait_ge(chunk_multiplied, Q["s1", l, 0] + 1)
                then(v.tensor_tensor(sm2(1, 8), B5v[:, :, 128:136], over(heads[:, R_DTB + 8 * l:R_DTB + 8 * l + 8], 2), ALU.add))
                v.scalar_tensor_tensor(out=sm(2), in0=sm(1), scalar=-1.0, in1=sm(1), op0=ALU.mult, op1=ALU.min).then_inc(d_x, 1)
                vb = VT[1, l]
                for i in range(13):
                    if i < 12:
                        conv(("qkv", l, i), 12 * l + i, 4, lambda tap, m: vcol[:, vb, 24 * tap + 2 * i + m:24 * tap + 2 * i + m + 1], None)
                    if i >= 1:
                        silu(12 * l + i - 1, qkv[:, 2 * i - 2:2 * i, :])
                dve.wait_ge(d_e, l + 1)
                then(v.scalar_tensor_tensor(out=sm(3), in0=sm(1), scalar=0.0, in1=sm(3), op0=ALU.max, op1=ALU.add),
                     v.tensor_scalar_add(sm(4), sm(4), 1.0))
                v.tensor_tensor(sm2(0, 8), sm2(3, 8), over(nea[:, 8 * l:8 * l + 8], 2), ALU.mult).then_inc(d_glog, 1)
                then(v.reciprocal(sm(4), sm(4)))
                dve.wait_ge(in_copied, INC["z", l, 3])
                sigmoid(ezb[:, :, :])
                then(v.tensor_tensor(zbuf[:, :, :], zbuf[:, :, :], ezb[:, :, :], ALU.mult))
                dve.wait_ge(in_copied, INC["ga", l, 3])
                sigmoid(gab[:, :, :])
                dve.wait_ge(in_copied, INC["gb", l, 3])
                sigmoid(gbb[:, :, :])
                dve.wait_ge(decay_sums, l + 1)
                v.tensor_copy(sm(5), B[5][:, 0:16]).then_inc(d_gcc, 1)
                dve.wait_ge(d_egc, l + 1)
                v.scalar_tensor_tensor(out=sm(7), in0=sm(4), scalar=-1.0, in1=sm(6), op0=ALU.mult, op1=ALU.mult).then_inc(d_coef, 1)
                rope([(swq[:, 2 * j:2 * j + 2, :], vc(0, l, VA["swa_q_norm"]), 2) for j in range(4)]
                     + [(kd[:, :, :], vc(0, l, VA["swa_k_norm"]), 2)], cosr[:, :], sinr[:, :])
                dve.wait_ge(rope_added, turned[0])
                gcc, beta, nbe, kc = sm2(5, 8), sm2(4, 8), sm2(7, 8), sm(8, 8)
                f4 = lambda ap: ap.rearrange("p (a b) -> p a b", a=4)

                def exponents(g):
                    c, h0 = g // 2, 4 * (g % 2)
                    dve.wait_ge(prep_done, 4 * l + g + 1)
                    if g >= 2:
                        dve.wait_ge(d_exp, 4 * l + g - 1)
                    gb_ = f4(B[3 * (g % 2)][:, :])
                    t1, tu, tl = f4(T1[:, g % 2, :]), f4(TU[:, g % 2, :]), f4(TL[:, g % 2, :])
                    ins = [v.tensor_tensor(t1, gb_, bcast(gcc[:, c, h0:h0 + 4], P), ALU.subtract)]
                    if c == 0:
                        ins.append(v.tensor_tensor(kc[:, h0:h0 + 4], gb_[:, :, P - 1], gcc[:, 0, h0:h0 + 4], ALU.subtract))
                    then(*ins)
                    then(v.tensor_tensor(tu, t1, over(k(C_MU), 4), ALU.add))
                    v.tensor_tensor(tl, over(k(C_ML), 4), t1, ALU.subtract).then_inc(d_exponent, 1)

                def rows(g):
                    c, h0 = g // 2, 4 * (g % 2)
                    dve.wait_ge(d_exp, 4 * l + g + 1)
                    b = 3 * (g % 2)
                    then(v.tensor_tensor(QM[:, g, :, :], f4(B[b + 1][:, :]), f4(TU[:, g % 2, :]), ALU.mult),
                         v.tensor_tensor(LL[:, g, :, :], f4(B[b + 2][:, :]), bcast(beta[:, c, h0:h0 + 4], P), ALU.mult))
                    if c == 1:
                        qd = QD[:, g - 2, :, :]
                        then(v.tensor_tensor(qd, qd, qkv[:, h0:h0 + 4, P:T], ALU.mult))
                    v.tensor_tensor(LL[:, g, :, :], LL[:, g, :, :], f4(TL[:, g % 2, :]), ALU.mult).then_inc(d_rows, 1)

                for g in range(5):
                    if g < 4:
                        exponents(g)
                    if g >= 1:
                        rows(g - 1)
                for s in range(LEVELS):
                    for g in range(4):
                        n = 4 * (LEVELS * l + s) + g
                        if s == 0:
                            dve.wait_ge(winv_done, n + 1)
                            then(v.tensor_tensor(Y[:, g, :, :], over(ident, 4), f4(B[g % 2][:, :]), ALU.subtract))
                            v.tensor_tensor(YT[:, g, :, :], over(ident, 4), LO[:, g, :, :], ALU.subtract).then_inc(y_updated, 1)
                            continue
                        dve.wait_ge(yinv_done, 4 * ((LEVELS - 1) * l + s - 1) + g + 1)
                        ins = [v.tensor_tensor(Y[:, g, :, :], Y[:, g, :, :], f4(B[2 + 2 * (g % 2)][:, :]), ALU.subtract)]
                        if s < LEVELS - 1:
                            then(*ins)
                            ins = [v.tensor_tensor(YT[:, g, :, :], YT[:, g, :, :], f4(B[3 + 2 * (g % 2)][:, :]), ALU.subtract)]
                        ins[0].then_inc(y_updated, 1)
                for g in range(4):
                    c, h0 = g // 2, 4 * (g % 2)
                    dve.wait_ge(kv_transposed, 4 * l + g + 1)
                    kcf = kc[:, h0:h0 + 4] if c == 0 else nbe[:, 1, h0:h0 + 4]
                    then(v.tensor_tensor(KX[:, g, :, :], f4(B[2 * (g % 2)][:, :]), bcast(kcf, P), ALU.mult))
                    v.tensor_tensor(VX[:, g, :, :], f4(B[2 * (g % 2) + 1][:, :]), bcast(beta[:, c, h0:h0 + 4], P), ALU.mult).then_inc(kv_ready, 1)
                places = [(U[:, 0], 0), (U[:, 1], 1), (WT[:, 0], 2), (WT[:, 1], 3), (S1[:, 0], 4), (S1[:, 1], 5), (oT[:, 0:4, 0:P], 0),
                          (oT[:, 4:8, 0:P], 1), (U[:, 2], 2), (U[:, 3], 3), (oT[:, 0:4, P:T], 4), (oT[:, 4:8, P:T], 5)]
                for n, (dst, b) in enumerate(places):
                    dve.wait_ge(step_done, 12 * l + n + 1)
                    v.tensor_copy(dst, f4(B[b][:, :])).then_inc(step_copied, 1)
                for i in range(4):
                    dve.wait_ge(out_factor, 4 * l + i + 1)
                    o = oT[:, 2 * i:2 * i + 2, :]
                    then(v.scalar_tensor_tensor(out=o, in0=o, scalar=vc(0, l, VA["dn_norm"]), in1=ORV[:, i, :].rearrange("p (m t) -> p m t", m=2),
                                                op0=ALU.mult, op1=ALU.mult))
                    ins = v.tensor_tensor(o, o, zbuf[:, 2 * i:2 * i + 2, :], ALU.mult)
                    if i < 3:
                        then(ins)
                    else:
                        ins.then_inc(out_normed, 1)
                attention(16, K[:, C_SWA:C_SWA + 384], heads[:, R_SINK + 16 * l:R_SINK + 16 * l + 16])
                for i in range(4):
                    key = ("dno", l, i)
                    dve.wait_ge(chunk_multiplied, Q[key] + 1)
                    v.tensor_tensor(mrg[:, 2 * i:2 * i + 2, :], LV[R[key] % 2], gab[:, 2 * i:2 * i + 2, :], ALU.mult).then_inc(merged, 1)
                for i in range(4):
                    key = ("swo", l, i)
                    dve.wait_ge(chunk_multiplied, Q[key] + 1)
                    y2 = yb[:, 2 * i:2 * i + 2, :]
                    then(v.tensor_tensor(y2, LV[R[key] % 2], gbb[:, 2 * i:2 * i + 2, :], ALU.mult))
                    v.tensor_tensor(mrg[:, 2 * i:2 * i + 2, :], mrg[:, 2 * i:2 * i + 2, :], y2, ALU.add).then_inc(merged, 1)
                for i in range(4):
                    key = ("wo", l, i)
                    dve.wait_ge(chunk_multiplied, Q[key] + 1)
                    for m in range(2):
                        t = 2 * i + m
                        v.scalar_tensor_tensor(out=x[:, t, :], in0=LV[R[key] % 2][:, m, :], scalar=modc[:, 16 + t:17 + t],
                                                   in1=x[:, t, :], op0=ALU.mult, op1=ALU.add).then_inc(x_done, 1)
                square(2 * l + 1, X0["ffn", l])
                scale(2 * l + 1, lambda t: scol[:, 8 + t:9 + t], True)
                vf = VT[2, l]
                for i in range(FP):
                    dve.wait_ge(chunk_multiplied, Q["ua", l, i] + 1)
                    if i >= 2:
                        dve.wait_ge(hidden_ready, FP * l + i - 1)
                    fa, fb, fc = FA[:, i % 2, :], FB[:, i % 2, :], FC[:, i % 2, :]
                    causal_taps(LV[R["ua", l, i] % 2], fb.rearrange("p (m t) -> p m t", m=2), 3,
                                lambda tap, m: vcol[:, vf, FT * tap + 2 * i + m:FT * tap + 2 * i + m + 1],
                                lambda m: vcol[:, vf, 66 + 2 * i + m:67 + 2 * i + m], fconv_done)
                    dve.wait_ge(ffn_exp, FP * l + i + 1)
                    sigmoid(fa)
                    then(v.tensor_tensor(fc, fa, fb, ALU.mult))
                    hidden(("ul", l, i), l, i, fc)
                dve.wait_ge(chunk_multiplied, Q["ud", l, FP - 1] + 1)
                for t in range(KT):
                    v.scalar_tensor_tensor(out=x[:, t, :], in0=B[t // 2][:, (t % 2) * T:(t % 2) * T + T], scalar=modc[:, 40 + t:41 + t],
                                               in1=x[:, t, :], op0=ALU.mult, op1=ALU.add).then_inc(x_done, 1)

            for l in range(LAYERS):
                ni, vd = 4 + 3 * l, VT[3, l]
                square(ni, X0["ffn1", l])
                scale(ni, lambda t: vcol[:, vd, t:t + 1], False)
                gated_ffn("g1", "u1", "d1", l, 2 + 2 * l, "ffn1")
                square(ni + 1, X0["out", l])
                scale(ni + 1, lambda t: vcol[:, vd, 8 + t:9 + t], False)
                dve.wait_ge(chunk_multiplied, Q["s2", l, 0] + 1)
                gb0 = heads[:, R_GB + 8 * l:R_GB + 8 * l + 8]
                then(v.tensor_tensor(sm2(1, 4), B5v[:, :, 68:72], over(gb0[:, 0:4], 2), ALU.add),
                     v.tensor_tensor(sm2(2, 4), B5v[:, :, 72:76], over(gb0[:, 4:8], 2), ALU.add),
                     v.tensor_copy(sm2(5, 4), B5v[:, :, 64:68]),
                     v.memset(vaug[:, :, :, 128:129], 1.0))
                v.scalar_tensor_tensor(out=sm(3, 8), in0=sm(2, 8), scalar=-1.0, in1=sm(2, 8), op0=ALU.mult, op1=ALU.min).then_inc(m_pre, 1)
                for i in range(5):
                    n = 24 + 4 * l + i
                    if i < 4:
                        conv(("qk", l, i), n, 4, lambda tap, m: vcol[:, vd, 24 + 8 * tap + 2 * i + m:25 + 8 * tap + 2 * i + m],
                             lambda m: vcol[:, vd, 56 + 2 * i + m:57 + 2 * i + m])
                    if i >= 1:
                        silu(n - 1, qkm[:, 2 * i - 2:2 * i, :])
                dve.wait_ge(m_l, l + 1)
                then(v.tensor_scalar(sm(6, 8), sm(2, 8), -1.0, 0.0, ALU.mult, ALU.max))
                v.tensor_tensor(sm(0, 8), sm(6, 8), sm(4, 8), ALU.add).then_inc(m_gates, 1)
                dve.wait_ge(in_copied, INC["om", l, 1])
                sigmoid(gab[:, 0:4, :])
                dve.wait_ge(silu_done, 24 + 4 * l + 4)
                rope([(swq[:, 0:2, :], vc(3, l, 64), 2), (swq[:, 2:4, :], vc(3, l, 64), 2), (swq[:, 4:6, :], None, 0),
                      (kd[:, :, :], vc(3, l, 65), 1)], K[:, C_COS2:C_COS2 + T], K[:, C_SIN2:C_SIN2 + T])
                wi = sm2(5, 4)
                for hh in range(4):
                    dve.wait_ge(index_done, 4 * l + hh + 1)
                    b = B[hh % 2]
                    dst = IX if hh == 0 else IT[:, hh % 2, :]
                    then(v.tensor_scalar(dst[:, 0:P], b[:, 0:P], 0.0, wi[:, 0, hh:hh + 1], ALU.max, ALU.mult))
                    v.tensor_scalar(dst[:, P:3 * P], b[:, P:3 * P], 0.0, wi[:, 1, hh:hh + 1], ALU.max, ALU.mult).then_inc(index_read, 1)
                    dve.wait_ge(index_read, 4 * l + hh + 1)
                    if hh:
                        then(v.tensor_tensor(IX, IX, dst, ALU.add))
                dve.wait_ge(m_sums, l + 1)
                nb, tot, acol, mc, m1, ca, em = sm2(19, 4), sm2(20, 4), sm2(18, 4), sm2(21, 4), sm(22, 4), sm(23, 4), sm(24, 8)
                then(v.tensor_copy(sm(19, 8), B[2][:, 0:8]), v.tensor_copy(sm(20, 8), B[2][:, 8:16]))
                v.tensor_tensor(sm(18, 8), sm(1, 8), sm(19, 8), ALU.add).then_inc(m_columns, 1)
                dve.wait_ge(m_columns, l + 1)
                dve.wait_ge(m_arc, l + 1)
                for c in range(2):
                    then(*[v.tensor_tensor_scan(mMR[:, c, j, :], mAR[:, c, j, :], mAR[:, c, j, :], m1[:, j:j + 1] if c else 0.0, ALU.max, ALU.max)
                           for j in range(4)])
                    if c == 0:
                        then(v.tensor_tensor(m1, mMR[:, 0, :, P - 1], tot[:, 0, :], ALU.subtract))
                f8 = lambda ap: ap.rearrange("p c h t -> p (c h) t")
                then(v.tensor_tensor(f8(mX), f8(mMR), over(ident, 8), ALU.mult),
                     v.tensor_tensor(f8(mT), over(k(C_MU), 8), f8(mMR), ALU.subtract),
                     v.tensor_tensor(ca, acol[:, 0, :], mMR[:, 0, :, P - 1], ALU.subtract))
                then(v.tensor_reduce(sm(21, 8), f8(mX), AXX, ALU.add))
                v.tensor_tensor(em, sm(19, 8), sm(21, 8), ALU.subtract).then_inc(m_masked, 1)
                dve.wait_ge(m_expd, l + 1)
                dve.wait_ge(m_keys, l + 1)
                v.scalar_tensor_tensor(out=mKX, in0=f4(B[5][:, :]), scalar=float(P) ** -0.5, in1=bcast(ca, P), op0=ALU.mult, op1=ALU.mult).then_inc(m_kx, 1)
                dve.wait_ge(m_scores, l + 1)
                then(*[v.scalar_tensor_tensor(out=mS[:, c, :, :], in0=f4(B[3 + c][:, :]), scalar=float(P) ** -0.5, in1=mT[:, c, :, :],
                                              op0=ALU.mult, op1=ALU.mult) for c in range(2)],
                     v.tensor_tensor(mQD, mQD, qkm[:, 0:4, P:T], ALU.mult))
                dve.wait_ge(m_state, l + 1)
                two = lambda b: b[:, :].rearrange("p (m t) -> p m t", m=2)
                then(v.tensor_copy(mCA[:, 0:2, 0:129], two(B[2])[:, :, 0:129]))
                v.tensor_copy(mCA[:, 2:4, 0:129], two(B[5])[:, :, 0:129]).then_inc(m_ca, 1)
                dve.wait_ge(m_nums, l + 1)
                den = sm(25, 8)
                nums = (B[3], B[4], B[0], B[1])
                then(*[v.tensor_copy(den[:, 2 * n:2 * n + 2], two(b)[:, :, 128]) for n, b in enumerate(nums)])
                then(v.tensor_scalar(sm(26, 8), den, -1.0, None, ALU.mult))
                then(v.tensor_tensor(den, den, sm(26, 8), ALU.max))
                then(v.tensor_tensor(den, den, em, ALU.max))
                then(v.reciprocal(den, den))
                then(*[v.tensor_tensor(f8(mH)[:, 2 * n:2 * n + 2, :], two(b)[:, :, 0:P], bcast(den[:, 2 * n:2 * n + 2], P), ALU.mult)
                       for n, b in enumerate(nums)])
                then(v.tensor_tensor(f8(mX), f8(mH), f8(mH), ALU.mult))
                v.tensor_reduce(sm(27, 8), f8(mX), AXX, ALU.add).then_inc(m_w, 1)
                dve.wait_ge(m_factor, l + 1)
                v.tensor_tensor(f8(mH), f8(mH), bcast(sm(27, 8), P), ALU.mult).then_inc(m_h, 1)
                then(v.tensor_tensor(IW, IX, K[:, C_CAUS:C_CAUS + 384], ALU.add))
                best = small[:, 16 * 28:16 * 28 + 16]
                for _ in range(TOPK // 8):
                    then(v.max(out=best[:, 0:8], in_=IW[:, 0:P]), v.max(out=best[:, 8:16], in_=IW[:, P:3 * P]))
                    then(v.match_replace(out=IW[:, 0:P], in_to_replace=best[:, 0:8], in_values=IW[:, 0:P], imm_value=-3e38),
                         v.match_replace(out=IW[:, P:3 * P], in_to_replace=best[:, 8:16], in_values=IW[:, P:3 * P], imm_value=-3e38))
                then(v.tensor_scalar(IM, IW, -2e38, NEG, ALU.is_gt, ALU.mult))
                then(v.tensor_tensor(IM, IM, K[:, C_CAUS:C_CAUS + 384], ALU.add))
                dve.wait_ge(m_turned, l + 1)
                for c in range(2):
                    for j in range(4):
                        ins = v.scalar_tensor_tensor(out=atT[:, 4 + j, c * P:(c + 1) * P], in0=B[2 if c == 0 else 5][:, j * P:(j + 1) * P],
                                                     scalar=vc(3, l, 66 + j), in1=gab[:, j, c * P:(c + 1) * P], op0=ALU.mult, op1=ALU.mult)
                        if (c, j) == (1, 3):
                            ins.then_inc(m_added, 1)
                        else:
                            then(ins)
                attention(8, IM, None)
                for i in range(4):
                    key = ("out", l, i)
                    dve.wait_ge(chunk_multiplied, Q[key] + 1)
                    xx = x[:, 2 * i:2 * i + 2, :]
                    v.tensor_tensor(xx, xx, LV[R[key] % 2], ALU.add).then_inc(x_done, 1)
                square(ni + 2, X0["ffn2", l])
                scale(ni + 2, lambda t: vcol[:, vd, 16 + t:17 + t], False)
                gated_ffn("g2", "u2", "d2", l, 3 + 2 * l, "ffn2")
            for u in range(4):
                dve.wait_ge(final_transposed, u + 1)
                v.tensor_copy(xin2[:, u // 2, 512 * (u % 2):512 * (u % 2) + 512], B[u][:, :]).then_inc(final_copied, 1)

        @block.scalar
        def _(act):
            a_ = nc.scalar.activation
            count = [0]

            def then(*ins):
                for i in ins:
                    i.then_inc(a_chain, 1)
                count[0] += len(ins)
                act.wait_ge(a_chain, count[0])

            def rsqrt(dst, src, scale, bias, name):
                then(a_(dst, src, ACT.Ln, bias=col(COL_EPS), scale=scale))
                a_(dst, dst, ACT.Exp, bias=bias, scale=-0.5).then_inc(name, 1)

            def norm(ni, shift):
                act.wait_ge(norm_sum, ni + 1)
                rsqrt(rinv[:, :], B[4][:, 0:T], 1.0 / D, 0.0, norm_factor)
                if shift is not None:
                    for t in range(KT):
                        act.wait_ge(norm_unbiased, KT * ni + t + 1)
                        a_(h[:, t, :], tmp[:, t, :], ACT.Identity, bias=modc[:, shift + t:shift + t + 1], scale=1.0).then_inc(norm_ready, 1)

            def exp_of_conv(n):
                act.wait_ge(conv_done, n + 1)
                if n >= 2:
                    act.wait_ge(silu_done, n - 1)
                a_(EV[:, n % 2, :], CV[:, n % 2, :], ACT.Exp, scale=-1.0).then_inc(conv_exp, 1)

            sums = [0]

            def rope(normed):
                for j, yes in enumerate(normed):
                    if yes:
                        n = sums[0]
                        act.wait_ge(rope_sum, n + 1)
                        rsqrt(RRV[:, j, :], B[n % 2][:, :], 1.0 / 64, 0.0, rope_factor)
                        sums[0] += 1

            lots, turned, pairs = [0], [0], [0]

            def attention(nh, sink):
                def exps(lot):
                    gl = lots[0] + lot
                    buf = gl % 2
                    act.wait_ge(rows_max, gl + 1)
                    nm, rs = sm2(10 + buf, 4), sm2(12 + buf, 4)
                    for b in range(2):
                        for h4 in range(4):
                            s = SP[:, buf, h4, 0:P] if b == 0 else SP[:, buf, h4, P:3 * P]
                            ins = a_(s, s, ACT.Exp, bias=nm[:, b, h4:h4 + 1], scale=1.0, accum_out=rs[:, b, h4:h4 + 1])
                            if (b, h4) == (1, 3) and not sink:
                                ins.then_inc(exp_done, 1)
                            else:
                                then(ins)
                    if sink:
                        a_(sm(14 + buf, 8), sm(14 + buf, 8), ACT.Exp).then_inc(exp_done, 1)

                def copies():
                    for _ in range(4):
                        n = turned[0]
                        act.wait_ge(probs_transposed, n + 1)
                        if n >= 2:
                            act.wait_ge(head_weighed, n - 1)
                        a_(PT[:, n % 2, :], B[3 + n % 2][:, 0:384], ACT.Copy).then_inc(probs_copied, 1)
                        turned[0] += 1
                        if turned[0] % 2 == 0 and turned[0] >= 2:
                            pair = pairs[0]
                            act.wait_ge(head_weighed, 2 * pair + 2)
                            a_(atT[:, pair % (nh // 2), :], L[pair % 2][:, 0:T], ACT.Copy).then_inc(pair_copied, 1)
                            pairs[0] += 1

                n = nh // 4
                exps(0)
                for lot in range(n):
                    if lot + 1 < n:
                        exps(lot + 1)
                    copies()
                lots[0] += n

            def exps_of(key, fi, i):
                act.wait_ge(chunk_multiplied, Q[key] + 1)
                if i >= 2:
                    act.wait_ge(hidden_ready, FP * fi + i - 1)
                a_(FA[:, i % 2, :], L[R[key] % 2][:, :], ACT.Exp, scale=-1.0).then_inc(ffn_exp, 1)

            act.wait_ge(start_v, 2)
            then(a_(modc[:, 0:KT], ccol[:, :], ACT.Exp, scale=-1.0))
            a_(nea[:, :], heads[:, R_ALOG:R_ALOG + 16], ACT.Exp).then_inc(start_a, 1)
            act.wait_ge(start_v, 3)
            then(a_(sinr[:, :], ta, ACT.Sin))
            a_(cosr[:, :], tc_, ACT.Sin, bias=col(COL_HPI), scale=-1.0).then_inc(start_a, 1)

            for l in range(LAYERS):
                norm(2 * l, 0)
                act.wait_ge(chunk_multiplied, Q["s1", l, 0] + 1)
                act.wait_ge(d_x, l + 1)
                then(a_(vtok[:, :, :], B[5][:, :].rearrange("p (c n) -> p c n", c=2)[:, :, 0:P], ACT.Copy),
                     a_(sm2(4, 8), B[5][:, :].rearrange("p (c n) -> p c n", c=2)[:, :, 136:144], ACT.Exp, scale=-1.0),
                     a_(sm(3), sm(2), ACT.Exp))
                a_(kd[:, :, :], LV[R["s1", l, 0] % 2], ACT.Copy).then_inc(in_copied, 1)
                a_(sm(3), sm(3), ACT.Ln, bias=col(COL_ONE), scale=1.0).then_inc(d_e, 1)
                for i in range(12):
                    exp_of_conv(12 * l + i)
                    if 3 <= i < 11:
                        n = 8 * l + i - 3
                        act.wait_ge(head_sum_done, n + 1)
                        if n >= 2:
                            act.wait_ge(head_normed, n - 1)
                        rsqrt(RV[:, n % 2, :], B[n % 2][:, :], 1.0, col(COL_QS) if i - 3 < 4 else 0.0, head_factor)
                for i in range(4):
                    act.wait_ge(chunk_multiplied, Q["swq", l, i] + 1)
                    a_(swq[:, 2 * i:2 * i + 2, :], LV[R["swq", l, i] % 2], ACT.Copy).then_inc(in_copied, 1)
                for i in range(4):
                    act.wait_ge(chunk_multiplied, Q["z", l, i] + 1)
                    then(a_(zbuf[:, 2 * i:2 * i + 2, :], LV[R["z", l, i] % 2], ACT.Copy))
                    a_(ezb[:, 2 * i:2 * i + 2, :], LV[R["z", l, i] % 2], ACT.Exp, scale=-1.0).then_inc(in_copied, 1)
                for kind, buf in (("ga", gab), ("gb", gbb)):
                    for i in range(4):
                        act.wait_ge(chunk_multiplied, Q[kind, l, i] + 1)
                        a_(buf[:, 2 * i:2 * i + 2, :], LV[R[kind, l, i] % 2], ACT.Exp, scale=-1.0).then_inc(in_copied, 1)
                act.wait_ge(d_gcc, l + 1)
                a_(sm(6), sm(5), ACT.Exp).then_inc(d_egc, 1)
                rope([True] * 5)
                for g in range(4):
                    act.wait_ge(d_exponent, 4 * l + g + 1)
                    tu, tl = TU[:, g % 2, :], TL[:, g % 2, :]
                    then(a_(tu, tu, ACT.Exp))
                    if g < 2:
                        kcs = sm(8, 8)[:, 4 * g:4 * g + 4]
                        then(a_(kcs, kcs, ACT.Exp))
                    else:
                        then(a_(QD[:, g - 2, :, :], B[3 * (g % 2)][:, :].rearrange("p (a b) -> p a b", a=4), ACT.Exp))
                    a_(tl, tl, ACT.Exp).then_inc(d_exp, 1)
                for s in range(1, LEVELS):
                    for g in range(4):
                        n = 4 * (LEVELS * l + s) + g
                        act.wait_ge(winv_done, n + 1)
                        if s >= 2:
                            act.wait_ge(yinv_done, 4 * ((LEVELS - 1) * l + s - 1) + g - 3)
                        a_(W[:, g, :, :], B[g % 2][:, :].rearrange("p (a b) -> p a b", a=4), ACT.Copy).then_inc(w_copied, 1)
                for i in range(4):
                    act.wait_ge(osum_done, 4 * l + i + 1)
                    rsqrt(ORV[:, i, :], B[i % 2][:, :], 1.0 / P, 0.0, out_factor)
                attention(16, True)
                norm(2 * l + 1, 24)
                for i in range(FP):
                    act.wait_ge(fconv_done, FP * l + i + 1)
                    if i >= 2:
                        act.wait_ge(hidden_ready, FP * l + i - 1)
                    a_(FA[:, i % 2, :], FB[:, i % 2, :], ACT.Exp, scale=-1.0).then_inc(ffn_exp, 1)

            for l in range(LAYERS):
                ni = 4 + 3 * l
                norm(ni, None)
                for i in range(FP):
                    exps_of(("g1", l, i), 2 + 2 * l, i)
                norm(ni + 1, None)
                act.wait_ge(chunk_multiplied, Q["s2", l, 0] + 1)
                act.wait_ge(m_pre, l + 1)
                then(a_(vtok[:, :, 0:64], B[5][:, :].rearrange("p (c n) -> p c n", c=2)[:, :, 0:64], ACT.Copy),
                     a_(sm(4, 8), sm(3, 8), ACT.Exp))
                a_(kd[:, :, :], LV[R["s2", l, 0] % 2], ACT.Copy).then_inc(in_copied, 1)
                a_(sm(4, 8), sm(4, 8), ACT.Ln, bias=col(COL_ONE), scale=1.0).then_inc(m_l, 1)
                for kind, n, t0 in (("aq", 2, 0), ("qi", 1, 4)):
                    for i in range(n):
                        act.wait_ge(chunk_multiplied, Q[kind, l, i] + 1)
                        a_(swq[:, t0 + 2 * i:t0 + 2 * i + 2, :], LV[R[kind, l, i] % 2], ACT.Copy).then_inc(in_copied, 1)
                for i in range(4):
                    exp_of_conv(24 + 4 * l + i)
                for i in range(2):
                    key = ("vm", l, i)
                    act.wait_ge(chunk_multiplied, Q[key] + 1)
                    src = LV[R[key] % 2].rearrange("p c (h e) -> p c h e", h=2)
                    then(a_(vaug[:, 0, 2 * i:2 * i + 2, 0:P], src[:, 0], ACT.Copy))
                    a_(vaug[:, 1, 2 * i:2 * i + 2, 0:P], src[:, 1], ACT.Copy).then_inc(in_copied, 1)
                for i in range(2):
                    key = ("om", l, i)
                    act.wait_ge(chunk_multiplied, Q[key] + 1)
                    a_(gab[:, 2 * i:2 * i + 2, :], LV[R[key] % 2], ACT.Exp, scale=-1.0).then_inc(in_copied, 1)
                rope([True, True, False, True])
                act.wait_ge(m_rows, l + 1)
                then(a_(mAR[:, 0, :, :], B[3][:, :].rearrange("p (a b) -> p a b", a=4), ACT.Copy))
                a_(mAR[:, 1, :, :], B[4][:, :].rearrange("p (a b) -> p a b", a=4), ACT.Copy).then_inc(m_arc, 1)
                act.wait_ge(m_masked, l + 1)
                acol, m1 = sm2(18, 4), sm(22, 4)
                then(*[a_(mT[:, c, j, :], mT[:, c, j, :], ACT.Exp, bias=acol[:, c, j:j + 1], scale=1.0) for c in range(2) for j in range(4)],
                     *[a_(mQD[:, j, :], mMR[:, 1, j, :], ACT.Exp, bias=m1[:, j:j + 1], scale=-1.0) for j in range(4)],
                     a_(sm(23, 4), sm(23, 4), ACT.Exp))
                a_(sm(24, 8), sm(24, 8), ACT.Exp).then_inc(m_expd, 1)
                act.wait_ge(m_w, l + 1)
                rsqrt(sm(27, 8), sm(27, 8), 1.0 / P, 0.0, m_factor)
                attention(8, False)
                norm(ni + 2, None)
                for i in range(FP):
                    exps_of(("g2", l, i), 3 + 2 * l, i)

        @block.gpsimd
        def _(pool):
            g_ = nc.gpsimd

            def rope_squares(pieces):
                for j, src, n in pieces:
                    pool.wait_ge(in_copied, n)
                    g_.tensor_tensor(RSQ[:, j, :].rearrange("p (m t) -> p m t", m=2), src, src, ALU.mult).then_inc(rope_squared, 1)

            for l in range(LAYERS):
                for i in range(11):
                    if i < 8:
                        n = 8 * l + i
                        pool.wait_ge(silu_done, 12 * l + i + 1)
                        if n >= 2:
                            pool.wait_ge(head_sum_done, n - 1)
                        qq = qkv[:, 2 * i:2 * i + 2, :]
                        g_.tensor_tensor(SV[:, n % 2, :].rearrange("p (m t) -> p m t", m=2), qq, qq, ALU.mult).then_inc(head_squared, 1)
                    if i >= 3:
                        n = 8 * l + i - 3
                        pool.wait_ge(head_factor, n + 1)
                        qq = qkv[:, 2 * i - 6:2 * i - 4, :]
                        g_.tensor_tensor(qq, qq, RV[:, n % 2, :].rearrange("p (m t) -> p m t", m=2), ALU.mult).then_inc(head_normed, 1)
                rope_squares([(j, swq[:, 2 * j:2 * j + 2, :], INC["swq", l, j]) for j in range(4)] + [(4, kd[:, :, :], INC["s1", l, 0])])
                for s in range(LEVELS):
                    for g in range(4):
                        if s == 0:
                            pool.wait_ge(d_rows, 4 * l + g + 1)
                        else:
                            pool.wait_ge(winv_done, 4 * (LEVELS * l + s - 1) + g + 1)
                        if s == 1:
                            pool.wait_ge(y_updated, 4 * LEVELS * l + g + 1)
                        g_.tensor_tensor(LO[:, g, :, :], LL[:, g, :, :], over(k(C_LV + s * P), 4), ALU.mult).then_inc(offdiag_ready, 1)
                pool.wait_ge(step_copied, 12 * l + 12)
                for i in range(4):
                    o = oT[:, 2 * i:2 * i + 2, :]
                    g_.tensor_tensor(OSQ[:, i, :].rearrange("p (m t) -> p m t", m=2), o, o, ALU.mult).then_inc(out_squared, 1)
            for l in range(LAYERS):
                rope_squares([(0, swq[:, 0:2, :], INC["aq", l, 0]), (1, swq[:, 2:4, :], INC["aq", l, 1]), (3, kd[:, :, :], INC["s2", l, 0])])


def kernel(**inputs):
    import concourse.bacc as bacc
    from concourse.bass_utils import run_bass_kernel_spmd

    nc = bacc.Bacc("TRN2", target_bir_lowering=False, num_devices=1)
    arrays, aps = {}, {}
    given = {n: np.ascontiguousarray(v) for n, v in inputs.items()}
    given["shape_constants"] = shape_constants()
    for name, value in given.items():
        arrays[f"in_{name}"] = value
        aps[name] = nc.dram_tensor(f"in_{name}", value.shape, mybir.dt.from_np(value.dtype), kind="ExternalInput").ap()
    out = nc.dram_tensor("out", (1, T, D), F32, kind="ExternalOutput").ap()
    build(nc, aps, out)
    result = run_bass_kernel_spmd(nc, [arrays], core_ids=[0])
    return result.results[0]["out"]
```

```python
from contextlib import ExitStack

import numpy as np
import concourse.bass as bass
from concourse import mybir

F32 = mybir.dt.float32
I32 = mybir.dt.int32
F32R = mybir.dt.float32r
ALU = mybir.AluOpType
ACT = mybir.ActivationFunctionType
AXX = mybir.AxisListType.X

P = 128
T = 256
D = 1024
KT = D // P
LAYERS = 2
DFF = 2816
FT = DFF // P
FP = FT // 2
EPS = 1e-6
NEG = -1e30
HD = 8
SLOT = KT * 272
NS = 3
TOPK = T // 4

C_IDENT, C_ONES, C_TRIU, C_BLK, C_PERM1, C_PERM2 = (i * P for i in range(6))
C_MU = 6 * P
C_LV = 7 * P
LEVELS = 7
C_COS2 = C_LV + LEVELS * P
C_SIN2 = C_COS2 + T
C_CAUS = C_SIN2 + T
C_SWA = C_CAUS + 2 * P
C_ML = C_CAUS
C_COL = C_SWA + 3 * P
COL_EPS, COL_QS, COL_INV, COL_HPI, COL_ONE, COL_KS = range(6)
C_ALL = C_COL + 8


def shape_constants():
    c = np.zeros((P, C_ALL), np.float32)
    i, j = np.arange(P)[:, None], np.arange(P)[None, :]
    c[:, C_IDENT:C_IDENT + P] = i == j
    c[:, C_ONES:C_ONES + P] = 1.0
    c[:, C_TRIU:C_TRIU + P] = i <= j
    c[:, C_BLK:C_BLK + P] = (i // 64) == (j // 64)
    for at, half in ((C_PERM1, 8), (C_PERM2, 32)):
        m = np.zeros((P, P), np.float32)
        for base in (0, 64):
            for r in range(half):
                m[base + r + half, base + r] = -1.0
                m[base + r, base + r + half] = 1.0
        c[:, at:at + P] = m
    c[:, C_MU:C_MU + P] = np.where(j >= i, 0.0, NEG)
    for s in range(LEVELS):
        w = 1 << s
        c[:, C_LV + s * P:C_LV + (s + 1) * P] = (i // (2 * w) == j // (2 * w)) & (i // w % 2 == 1) & (j // w % 2 == 0)
    inv2 = (10000.0 ** (-np.arange(32, dtype=np.float32) / np.float32(32))).astype(np.float32)
    ang = (np.arange(T, dtype=np.float32)[None, :] * inv2[np.arange(P) % 32][:, None]).astype(np.float32)
    c[:, C_COS2:C_COS2 + T] = np.cos(ang)
    c[:, C_SIN2:C_SIN2 + T] = np.sin(ang)
    c[:, C_SWA:C_SWA + P] = np.where(j <= i, 0.0, NEG)
    c[:, C_SWA + P:C_SWA + 2 * P] = np.where(j > i, 0.0, NEG)
    c[:, C_SWA + 2 * P:C_SWA + 3 * P] = np.where(j <= i, 0.0, NEG)
    c[:, C_CAUS:C_CAUS + P] = np.where(j <= i, 0.0, NEG)
    c[:, C_CAUS + 2 * P:C_CAUS + 3 * P] = np.where(j <= i, 0.0, NEG)
    inv1 = (500000.0 ** (-np.arange(8, dtype=np.float32) / np.float32(8))).astype(np.float32)
    lane = np.arange(P) % 64
    c[:, C_COL + COL_EPS] = EPS
    c[:, C_COL + COL_QS] = np.log(128.0 ** -0.5)
    c[:, C_COL + COL_INV] = np.where(lane < 16, inv1[lane % 8], 0.0)
    c[:, C_COL + COL_HPI] = np.pi / 2
    c[:, C_COL + COL_ONE] = 1.0
    return c


VA = dict(b_ada=0, norm_mix=48, norm_ffn=56, dn_norm=64, swa_q_norm=65, swa_k_norm=66)
VB = dict(dn_conv=0)
VC = dict(ffn_conv=0, ffn_conv_b=66)
VD = dict(ffn1_norm_2=0, mix_norm_2=8, ffn2_norm_2=16, conv_w_2=24, conv_b_2=56, q_norm_2=64, k_norm_2=65, m_norm_2=66)
V_ROWS = (67, 96, 88, 70)
R_ALOG, R_DTB, R_SINK, R_GB, R_ALL = 0, 16, 32, 64, 80


def schedule():
    out = []

    def ffn(kind_a, kind_b, kind_d, l, ada=None):
        for i in range(FP + 1):
            if i < FP:
                out.append((kind_a, l, i))
                out.append((kind_b, l, i))
            if ada is not None:
                out.extend(("ada", ada, 2 * i + m) for m in range(2))
            if i >= 1:
                out.append((kind_d, l, i - 1))

    for l in range(LAYERS):
        if l == 0:
            out.extend(("ada", 0, i) for i in range(24))
        out.append(("s1", l, 0))
        for kind, n in (("qkv", 12), ("z", 4), ("ga", 4), ("gb", 4), ("swq", 4), ("dno", 4), ("swo", 4), ("wo", 4)):
            out.extend((kind, l, i) for i in range(n))
        ffn("ua", "ul", "ud", l, ada=l + 1 if l + 1 < LAYERS else None)
    for l in range(LAYERS):
        ffn("g1", "u1", "d1", l)
        out.append(("s2", l, 0))
        for kind, n in (("aq", 2), ("qi", 1), ("qk", 4), ("vm", 2), ("om", 2), ("out", 4)):
            out.extend((kind, l, i) for i in range(n))
        ffn("g2", "u2", "d2", l)
    return out


def build(nc, a, out):
    chunks = schedule()
    Q = {key: q for q, key in enumerate(chunks)}
    unbanked = ("ada", "ud", "d1", "d2")
    M, M_OF, n_m, n_ada = {}, [], 0, 0
    SI, SPLIT, WHOLE = {}, [], ("s1", "s2", "vm", "dno", "swo", "wo", "out")
    for key in chunks:
        if key[0] == "ada":
            n_ada += 1
            M_OF.append(("modulated", n_ada))
        else:
            M[key] = n_m
            n_m += 1
            if key[0] in WHOLE:
                M_OF.append(("multiplied", n_m))
            else:
                SI[key] = len(SPLIT)
                SPLIT.append(key)
                M_OF.append(("split", len(SPLIT)))
    R = {key: r for r, key in enumerate(k for k in chunks if k[0] not in unbanked)}

    with ExitStack() as ctx:
        def sb(name, *shape, dt=F32):
            return ctx.enter_context(nc.sbuf_tensor(name, list(shape), dt))

        bank = [ctx.enter_context(nc.psum_tensor(f"bank{i}", [P, 512], F32)) for i in range(8)]
        L, B = bank[0:2], bank[2:8]
        LV = [b[:, :].rearrange("p (m t) -> p m t", m=2) for b in L]

        K = sb("constants", P, C_ALL)
        x = sb("x", P, KT, T)
        h = sb("h", P, KT, T)
        ring = [sb(f"ring{i}", P, SLOT) for i in range(NS)]
        vcol = sb("vcol", P, 8, P)
        heads = sb("heads", P, R_ALL)
        nea = sb("nea", P, 16)
        ccol = sb("ccol", P, KT)
        modc = sb("modc", P, 48)
        scol = sb("scol", P, 16)
        cosr = sb("cosr", P, T)
        sinr = sb("sinr", P, T)
        h_high = sb("h_high", P, KT, T, dt=F32R)
        rinv = sb("rinv", P, T)
        ARENA = 23552
        arena = sb("arena", P, ARENA)
        arena_at = nc.sbuf_base - 4 * ARENA

        def rounded(name, at, *shape):
            return nc.alloc_sbuf_tensor_at(name, [P] + list(shape), F32R, offset=arena_at + 4 * at)

        zbuf = sb("zbuf", P, KT, T)
        gab = sb("gab", P, KT, T)
        gbb = sb("gbb", P, KT, T)
        swq = sb("swq", P, KT, T)
        kd = sb("kd", P, 2, T)
        vtok = sb("vtok", P, 2, P)
        small = sb("small", P, 512)

        def ar(at, *shape):
            n = int(np.prod(shape))
            v = arena[:, at:at + n]
            if len(shape) == 2:
                return v.rearrange("p (a b) -> p a b", a=shape[0])
            if len(shape) == 3:
                return v.rearrange("p (a b c) -> p a b c", a=shape[0], b=shape[1])
            return v

        qkv = ar(0, 24, T)
        QM, LL, LO = ar(6144, 4, 4, P), ar(8192, 4, 4, P), ar(10240, 4, 4, P)
        Y, YT, W = ar(12288, 4, 4, P), ar(14336, 4, 4, P), ar(16384, 4, 4, P)
        KX, VX, QD = ar(18432, 4, 4, P), ar(20480, 4, 4, P), ar(22528, 2, 4, P)
        U, S1, WT, oT = ar(8192, 4, 4, P), ar(14336, 2, 4, P), ar(16384, 2, 4, P), ar(10240, HD, T)
        OSQ, ORV = ar(12288, 4, 512), ar(14336, 4, 512)
        CV, RV = ar(10240, 2, 512), ar(11264, 2, 512)
        T1, TU, TL = ar(16384, 2, 512), ar(17408, 2, 512), ar(18432, 2, 512)
        RSQ, RRV, rtmp = ar(16384, 5, 512), ar(19456, 5, 512), ar(12288, 512)
        xin2 = ar(6144, 2, D)
        h_low = rounded("h_low", 12288, KT, T)
        WH = [rounded(f"weights_high{i}", 14336 + 4096 * i, KT, T) for i in range(2)]
        WL = [rounded(f"weights_low{i}", 16384 + 4096 * i, KT, T) for i in range(2)]
        hidH, hidL = rounded("hidden_high", 0, 3, 512), rounded("hidden_low", 1536, 3, 512)
        HT = ar(3072, 2, 512)
        acc = ar(6144, 6 * D)
        HSQ = ar(6144, 8, 512)
        tmp = ar(4096, KT, T)
        SP = ar(0, 2, 4, 384)
        PT = ar(3072, 2, 384)
        atT = ar(12288, KT, T)
        FA, FB = ar(4096, 2, 512), ar(5120, 2, 512)
        mrg, yb = ar(0, KT, T), ar(2048, KT, T)
        qkm = ar(0, KT, T)
        vaug = ar(2048, 2, 4, 132)
        mAR, mMR, mT = ar(4096, 2, 4, P), ar(5120, 2, 4, P), ar(6144, 2, 4, P)
        mQD, mKX, mCA = ar(7168, 4, P), ar(7680, 4, P), ar(8192, 4, 132)
        mS, mH, mX = ar(9216, 2, 4, P), ar(10240, 2, 4, P), ar(11264, 2, 4, P)
        zf = zbuf[:, :, :].rearrange("p a b -> p (a b)")
        IX, IW, IM = zf[:, 0:384], zf[:, 384:768], zf[:, 768:1152]
        IT = zf[:, 1152:1920].rearrange("p (a b) -> p a b", a=2)
        rowst = ar(0, 8, P)
        xin = ar(1024, 2, D)
        crow, hrow = ar(3072, P), ar(3200, P)
        posf, ta, tb_, tc_ = (ar(22528 + 256 * i, T) for i in range(4))
        posi = sb("posi", 1, T, dt=I32)

        def sm(i, n=16):
            return small[:, 16 * i:16 * i + n]

        def sm2(i, heads_):
            return small[:, 16 * i:16 * i + 2 * heads_].rearrange("p (c h) -> p c h", c=2)

        def k(at, n=P):
            return K[:, at:at + n]

        def col(i):
            return K[:, C_COL + i:C_COL + i + 1]

        ident, ones = k(C_IDENT), k(C_ONES)

        def vc(tile, l, row):
            return vcol[:, VT[tile, l], row:row + 1]

        VT = {(t_, l): (3 * l + t_ if t_ < 3 else 6 + l) for t_ in range(4) for l in range(LAYERS)}

        def bcast(v, n):
            return v.unsqueeze(2).to_broadcast([P, v.shape[1], n])

        def over(v, n):
            return v.unsqueeze(1).to_broadcast([P, n, v.shape[1]])

        def sem(name):
            return ctx.enter_context(nc.semaphore(name))

        inputs_landed = sem("inputs_landed")
        output_stored = sem("output_stored")
        chunk_multiplied = sem("chunk_multiplied")
        start_transposed = sem("start_transposed")
        norm_sum = sem("norm_sum")
        mod_summed = sem("mod_summed")
        head_sum_done = sem("head_sum_done")
        decay_sums = sem("decay_sums")
        prep_done = sem("prep_done")
        winv_done = sem("winv_done")
        yinv_done = sem("yinv_done")
        kv_transposed = sem("kv_transposed")
        step_done = sem("step_done")
        osum_done = sem("osum_done")
        rope_sum = sem("rope_sum")
        rope_turned = sem("rope_turned")
        scores_done = sem("scores_done")
        probs_transposed = sem("probs_transposed")
        head_weighed = sem("head_weighed")
        final_transposed = sem("final_transposed")
        index_done = sem("index_done")
        m_sums = sem("m_sums")
        m_rows = sem("m_rows")
        m_keys = sem("m_keys")
        m_scores = sem("m_scores")
        m_state = sem("m_state")
        m_nums = sem("m_nums")
        m_turned = sem("m_turned")
        vector_order = sem("vector_order")
        scalar_order = sem("scalar_order")
        pool_order = sem("pool_order")
        start_v = sem("start_v")
        squares_ready = sem("squares_ready")
        norm_ready = sem("norm_ready")
        conv_done = sem("conv_done")
        chunk_modulated = sem("chunk_modulated")
        chunk_split = sem("chunk_split")
        h_scaled = sem("h_scaled")
        hid_whole = sem("hid_whole")
        d_x = sem("d_x")
        d_glog = sem("d_glog")
        d_gcc = sem("d_gcc")
        d_coef = sem("d_coef")
        d_exponent = sem("d_exponent")
        d_rows = sem("d_rows")
        y_updated = sem("y_updated")
        kv_ready = sem("kv_ready")
        step_copied = sem("step_copied")
        rope_normed = sem("rope_normed")
        rope_added = sem("rope_added")
        rows_masked = sem("rows_masked")
        rows_max = sem("rows_max")
        probs_ready = sem("probs_ready")
        merged = sem("merged")
        hidden_ready = sem("hidden_ready")
        fconv_done = sem("fconv_done")
        x_done = sem("x_done")
        m_gates = sem("m_gates")
        m_columns = sem("m_columns")
        m_masked = sem("m_masked")
        m_kx = sem("m_kx")
        m_w = sem("m_w")
        m_ca = sem("m_ca")
        m_h = sem("m_h")
        m_added = sem("m_added")
        m_pre = sem("m_pre")
        index_read = sem("index_read")
        final_copied = sem("final_copied")
        start_a = sem("start_a")
        norm_factor = sem("norm_factor")
        silu_done = sem("silu_done")
        chunk_rounded = sem("chunk_rounded")
        h_rounded = sem("h_rounded")
        hid_rounded = sem("hid_rounded")
        head_factor = sem("head_factor")
        d_e = sem("d_e")
        d_egc = sem("d_egc")
        d_exp = sem("d_exp")
        w_copied = sem("w_copied")
        in_copied = sem("in_copied")
        out_factor = sem("out_factor")
        rope_factor = sem("rope_factor")
        exp_done = sem("exp_done")
        probs_copied = sem("probs_copied")
        pair_copied = sem("pair_copied")
        ffn_act = sem("ffn_act")
        m_l = sem("m_l")
        m_arc = sem("m_arc")
        m_expd = sem("m_expd")
        m_factor = sem("m_factor")
        head_squared = sem("head_squared")
        head_normed = sem("head_normed")
        offdiag_ready = sem("offdiag_ready")
        out_squared = sem("out_squared")
        out_normed = sem("out_normed")
        rope_squared = sem("rope_squared")
        w_landed = [ctx.enter_context(nc.semaphore(f"weights_landed{i}")) for i in range(NS)]
        v_chain, a_chain = vector_order, scalar_order

        xs = [("x", 0, 4)] + [(n, l, 8) for l in range(LAYERS) for n in ("wo", "ffn")] \
            + [(n, l, 4) for l in range(LAYERS) for n in ("ffn1", "out", "ffn2")]
        X0, total_x, x_steps = {}, 0, []
        for n, l, c in xs:
            X0[n, l] = total_x
            x_steps.append([total_x + (u + 1) * c // 4 for u in range(4)])
            total_x += c

        def release(key):
            kind, l, i = key
            if kind in ("s1", "s2"):
                return in_copied, INC[key]
            if kind == "qkv":
                return conv_done, 12 * l + i + 1
            if kind == "qk":
                return conv_done, 24 + 4 * l + i + 1
            if kind in ("swq", "z", "ga", "gb", "aq", "qi", "vm", "om"):
                return in_copied, INC[key]
            if kind in ("dno", "swo"):
                return merged, 8 * l + 4 * (kind == "swo") + i + 1
            if kind == "wo":
                return x_done, X0["wo", l] + 2 * i + 2
            if kind == "out":
                return x_done, X0["out", l] + i + 1
            if kind == "ua":
                return fconv_done, FP * l + i + 1
            fi = {"ul": l, "g1": 2 + 2 * l, "u1": 2 + 2 * l, "g2": 3 + 2 * l, "u2": 3 + 2 * l}[kind]
            if kind[0] == "g":
                return ffn_act, FP * fi + i + 1
            return hidden_ready, FP * fi + i + 1

        INC, n_inc = {}, 0
        for key in chunks:
            if key[0] in ("s1", "s2", "swq", "z", "ga", "gb", "aq", "qi", "vm", "om"):
                n_inc += 1
                INC[key] = n_inc
        by_turn = {r: key for key, r in R.items()}

        block = ctx.enter_context(nc.Block())

        def slot(q):
            return ring[q % NS]

        wname = dict(ua="w_up", ul="w_up", g1="ffn1_w_gate_2", u1="ffn1_w_up_2", g2="ffn2_w_gate_2", u2="ffn2_w_up_2",
                     ud="w_down", d1="ffn1_w_down_2", d2="ffn2_w_down_2", ada="w_ada", dno="w_dn_out", swo="w_swa_out",
                     wo="w_o", out="w_out_2")
        wcol = dict(qkv=0, z=3072, swq=4112, ga=5392, gb=6416, ul=DFF)
        wcol2 = dict(aq=0, qi=640, qk=964, vm=1988, om=2500)
        S1_COLS = ((0, 5136, 256), (256, 4096, 16))
        S2_COLS = ((0, 512, 64), (64, 896, 64), (128, 576, 64), (192, 960, 4), (196, 3012, 8))

        N_IN = 4 + LAYERS * (8 + 1 + 2 + 10) + 4
        landed = {}
        total = [0] * NS
        for q, (kind, _, _) in enumerate(chunks):
            total[q % NS] += 16 * (len(S1_COLS) if kind == "s1" else len(S2_COLS) if kind == "s2" else 1)
            landed[q] = total[q % NS]

        @block.sync
        def _(sp):
            n_in = [0]

            def load(dst, src):
                sp.dma_start(dst, src).then_inc(inputs_landed, 16)
                n_in[0] += 1

            load(K[:, :], a["shape_constants"])
            load(xin[:, :, :], a["x"][0].rearrange("(b p) d -> p b d", p=P))
            load(crow[0:KT, :], a["c"].rearrange("a (k p) -> (a k) p", p=P))
            load(posi[:, :], a["positions"])
            for l in range(LAYERS):
                for tile, rows in ((0, VA), (1, VB), (2, VC), (3, VD)):
                    for name, r0 in rows.items():
                        src = a[name][l]
                        if name in ("swa_q_norm", "swa_k_norm", "q_norm_2", "k_norm_2"):
                            src = src.rearrange("(a n) -> a n", a=1)
                            load(rowst[r0:r0 + 1, VT[tile, l], 0:64], src)
                            load(rowst[r0:r0 + 1, VT[tile, l], 64:128], src)
                            continue
                        if name == "conv_w_2":
                            src = src.rearrange("k a (j p) -> (k a j) p", p=P)
                        elif name == "m_norm_2":
                            pass
                        elif len(src.shape) == 2:
                            src = src.rearrange("k (j p) -> (k j) p", p=P)
                        else:
                            src = src.rearrange("(j p) -> j p", p=P)
                        load(rowst[r0:r0 + src.shape[0], VT[tile, l], :], src)
            for at, name, n in ((R_ALOG, "dn_a_log", 16), (R_DTB, "dn_dt_bias", 16), (R_SINK, "swa_sinks", 32), (R_GB, "gate_b_2", 16)):
                load(hrow[0:1, at:at + n], a[name].rearrange("(o l) n -> o (l n)", o=1))
            assert n_in[0] == N_IN, n_in

            for q, (kind, l, i) in enumerate(chunks):
                if q >= NS:
                    use, n_used = M_OF[q - NS]
                    if use == "multiplied":
                        sp.wait_ge(chunk_multiplied, n_used)
                    elif use == "split":
                        sp.wait_ge(chunk_split, n_used)
                    else:
                        sp.wait_ge(chunk_modulated, n_used)
                s = slot(q)
                if kind in ("s1", "s2"):
                    w = a["w_in" if kind == "s1" else "w_in_2"][l].rearrange("(t p) n -> p t n", p=P)
                    dst = s[:, :].rearrange("p (t n) -> p t n", t=KT)
                    for at, c0, n in (S1_COLS if kind == "s1" else S2_COLS):
                        sp.dma_start(dst[:, :, at:at + n], w[:, :, c0:c0 + n]).then_inc(w_landed[q % NS], 16)
                    continue
                if kind in ("ud", "d1", "d2"):
                    w = a[wname[kind]][l].rearrange("(t p) n -> p t n", p=P)
                    sp.dma_start(s[:, 0:2 * D].rearrange("p (t n) -> p t n", t=2), w[:, 2 * i:2 * i + 2, :]).then_inc(w_landed[q % NS], 16)
                    continue
                if kind in wcol2:
                    w, c0 = a["w_in_2"], wcol2[kind]
                elif kind in ("qkv", "z", "swq", "ga", "gb"):
                    w, c0 = a["w_in"], wcol[kind]
                else:
                    w, c0 = a[wname[kind]], wcol.get(kind, 0)
                c0 += 256 * i
                sp.dma_start(s[:, 0:2 * D].rearrange("p (t n) -> p t n", t=KT),
                             w[l].rearrange("(t p) n -> p t n", p=P)[:, :, c0:c0 + 256]).then_inc(w_landed[q % NS], 16)
            sp.wait_ge(final_copied, 4)
            sp.dma_start(out[0].rearrange("(b p) d -> p b d", p=P), xin2[:, :, :]).then_inc(output_stored, 16)
            sp.wait_ge(output_stored, 16)

        @block.tensor
        def _(pe):
            mm, tr = nc.tensor.matmul, nc.tensor.transpose
            cnt = dict(rs=0, rp=0, sc=0, pt=0, pv=0, lot=0)

            def arrive(key):
                q = Q[key]
                pe.wait_ge(w_landed[q % NS], landed[q])
                if key in R and R[key] >= 2:
                    pe.wait_ge(*release(by_turn[R[key] - 2]))
                return slot(q)[:, 0:2 * D].rearrange("p (t n) -> p t n", t=KT)

            def linear3(key, high, low, norm=None):
                n = SI[key]
                wh, wl = WH[n % 2], WL[n % 2]
                pe.wait_ge(chunk_split, n + 1)
                if R[key] >= 2:
                    pe.wait_ge(*release(by_turn[R[key] - 2]))
                o = LV[R[key] % 2]
                for m in range(2):
                    for t in range(KT):
                        if norm is not None and m == 0:
                            pe.wait_ge(norm_ready, KT * norm + t + 1)
                        a_, b_ = wh[:, t, m * P:(m + 1) * P], wl[:, t, m * P:(m + 1) * P]
                        mm(o[:, m, :], a_, high[:, t, :], start=(t == 0), stop=False)
                        mm(o[:, m, :], a_, low[:, t, :], start=False, stop=False)
                        last = mm(o[:, m, :], b_, high[:, t, :], start=False, stop=(t == KT - 1))
                last.then_inc(chunk_multiplied, 1)

            def linear(key, rhs, norm=None):
                w = arrive(key)
                o = LV[R[key] % 2]
                for m in range(2):
                    for t in range(KT):
                        if norm is not None and m == 0:
                            pe.wait_ge(norm_ready, KT * norm + t + 1)
                        last = mm(o[:, m, :], w[:, t, m * P:(m + 1) * P], rhs[:, t, :], start=(t == 0), stop=(t == KT - 1))
                last.then_inc(chunk_multiplied, 1)

            def sum_squares(ni):
                for t in range(KT):
                    if t % 2 == 0:
                        pe.wait_ge(squares_ready, 4 * ni + t // 2 + 1)
                    last = mm(B[4][:, 0:T], ones, tmp[:, t, :], start=(t == 0), stop=(t == KT - 1))
                last.then_inc(norm_sum, 1)

            def token_major(rhs_of, dst):
                for tt in range(2):
                    for t in range(KT):
                        last = mm(dst(tt), h[:, t, tt * P:(tt + 1) * P], rhs_of(t), start=(t == 0), stop=(t == KT - 1))
                return last

            def special(kind, l, ni):
                key = (kind, l, 0)
                arrive(key)
                w = slot(Q[key])[:, :].rearrange("p (t n) -> p t n", t=KT)
                o = LV[R[key] % 2]
                pe.wait_ge(norm_ready, KT * ni + KT)
                for m in range(2):
                    for half in range(2):
                        for t in range(KT):
                            mm(o[64 * half:64 * half + 64, m, :], w[:, t, 64 * m:64 * m + 64], h[:, t, :],
                               start=(t == 0), stop=(t == KT - 1))
                n = 144 if kind == "s1" else 76
                token_major(lambda t: w[:, t, 128:128 + n], lambda tt: B[5][:, tt * T:tt * T + n]).then_inc(chunk_multiplied, 1)

            def rope(src, normed, perm):
                for j, yes in enumerate(normed):
                    if yes:
                        n = cnt["rs"]
                        pe.wait_ge(rope_squared, n + 1)
                        if n >= 2:
                            pe.wait_ge(rope_factor, n - 1)
                        mm(B[n % 2][:, :], k(C_BLK), RSQ[:, j, :], start=True, stop=True).then_inc(rope_sum, 1)
                        cnt["rs"] += 1
                n0 = cnt["rs"] - sum(normed)
                for j, yes in enumerate(normed):
                    if yes:
                        n0 += 1
                        pe.wait_ge(rope_normed, n0)
                    n = cnt["rp"]
                    if n >= 2:
                        pe.wait_ge(rope_added, n - 1)
                    mm(B[2 + n % 2][:, :], k(perm), src[j], start=True, stop=True).then_inc(rope_turned, 1)
                    cnt["rp"] += 1

            def attention(nh, qt, g_of, v_of):
                def scores(lot):
                    for h4 in range(4):
                        hh, n = 4 * lot + h4, cnt["sc"]
                        if n >= 3:
                            pe.wait_ge(rows_masked, n - 2)
                        b, lo = B[n % 3], 64 * (hh % 2)
                        kk = kd[lo:lo + 64, g_of(hh), :]
                        mm(b[:, 0:P], qt[lo:lo + 64, hh // 2, 0:P], kk[:, 0:P], start=True, stop=True)
                        mm(b[:, P:3 * P], qt[lo:lo + 64, hh // 2, P:T], kk, start=True, stop=True).then_inc(scores_done, 1)
                        cnt["sc"] += 1

                def turn(buf, h4):
                    n = cnt["pt"]
                    if n >= 2:
                        pe.wait_ge(probs_copied, n - 1)
                    for s in range(3):
                        last = tr(B[3 + n % 2][:, s * P:(s + 1) * P], SP[:, buf, h4, s * P:(s + 1) * P], ident)
                    last.then_inc(probs_transposed, 1)
                    cnt["pt"] += 1

                def weigh(hh, n):
                    pe.wait_ge(probs_copied, n + 1)
                    pair = cnt["pv"] // 2
                    if hh % 2 == 0 and pair >= 2:
                        pe.wait_ge(pair_copied, pair - 1)
                    o = L[pair % 2][64 * (hh % 2):64 * (hh % 2) + 64, 0:T]
                    pp = PT[:, n % 2, :]
                    mm(o[:, 0:P], v_of(hh, 0), pp[:, 0:P], start=True, stop=True)
                    mm(o[:, P:T], v_of(hh, 0), pp[:, P:2 * P], start=True, stop=False)
                    mm(o[:, P:T], v_of(hh, 1), pp[:, 2 * P:3 * P], start=False, stop=True).then_inc(head_weighed, 1)
                    cnt["pv"] += 1

                scores(0)
                for lot in range(nh // 4):
                    if lot + 1 < nh // 4:
                        scores(lot + 1)
                    pe.wait_ge(probs_ready, cnt["lot"] + 1)
                    n0 = cnt["pt"]
                    turn(cnt["lot"] % 2, 0)
                    for h4 in range(4):
                        if h4 < 3:
                            turn(cnt["lot"] % 2, h4 + 1)
                        weigh(4 * lot + h4, n0 + h4)
                    cnt["lot"] += 1

            def ffn(ka, kb, kc, l, ni, fi):
                for i in range(FP + 1):
                    if i < FP:
                        linear3((ka, l, i), h_high, h_low, norm=ni if i == 0 else None)
                        linear3((kb, l, i), h_high, h_low)
                    if i >= 1:
                        down(kc, l, i - 1, fi)

            def down(kc, l, i, fi):
                n = SI[kc, l, i]
                pe.wait_ge(chunk_split, n + 1)
                pe.wait_ge(hidden_ready, FP * fi + i + 1)
                wh, wl = (w[n % 2][:, :, :].rearrange("p a b -> p (a b)") for w in (WH, WL))
                for t in range(2):
                    for m in range(KT):
                        o = B[m // 2][:, (m % 2) * T:(m % 2) * T + T]
                        cols = slice(t * D + m * P, t * D + (m + 1) * P)
                        high, low = hidH[:, i % 3, t * T:(t + 1) * T], hidL[:, i % 3, t * T:(t + 1) * T]
                        mm(o, wh[:, cols], high, start=(i == 0 and t == 0 and m % 2 == 0), stop=False, skip_group_check=True)
                        mm(o, wh[:, cols], low, start=False, stop=False, skip_group_check=True)
                        last = mm(o, wl[:, cols], high, start=False, stop=(i == FP - 1 and t == 1), skip_group_check=True)
                last.then_inc(chunk_multiplied, 1)

            pe.wait_ge(inputs_landed, 16 * N_IN)
            for v in range(8):
                n = V_ROWS[v % 3] if v < 6 else V_ROWS[3]
                tr(B[v // 4][:, (v % 4) * P:(v % 4) * P + n], rowst[0:n, v, :], ident[0:n, 0:n])
            tr(B[2][:, 0:KT], crow[0:KT, :], ident[0:KT, 0:KT])
            mm(B[2][:, P:P + R_ALL], ones[0:1, :], hrow[0:1, 0:R_ALL], start=True, stop=True)
            pe.wait_ge(start_v, 1)
            mm(B[2][:, T:2 * T], ones[0:1, :], posf[0:1, :], start=True, stop=True).then_inc(start_transposed, 1)
            for u, b in enumerate((B[3], B[4], B[5], L[0])):
                for m in range(2):
                    for tt in range(2):
                        last = tr(b[:, m * T + tt * P:m * T + (tt + 1) * P], xin[:, tt, (2 * u + m) * P:(2 * u + m + 1) * P], ident)
                last.then_inc(start_transposed, 1)

            for l in range(LAYERS):
                if l == 0:
                    pe.wait_ge(start_v, 4)
                sum_squares(2 * l)
                pe.wait_ge(chunk_modulated, 24 * (l + 1))
                for m in range(48):
                    last = mm(B[5][:, m:m + 1], acc[:, m * P:(m + 1) * P], ones[:, 0:1], start=True, stop=True)
                last.then_inc(mod_summed, 1)
                special("s1", l, 2 * l)
                for i in range(12):
                    linear3(("qkv", l, i), h_high, h_low)
                for kind in ("z", "ga", "gb"):
                    for i in range(4):
                        linear3((kind, l, i), h_high, h_low)
                for i in range(4):
                    linear3(("swq", l, i), h_high, h_low)
                    for n in (8 * l + 2 * i, 8 * l + 2 * i + 1):
                        pe.wait_ge(head_squared, n + 1)
                        if n >= 2:
                            pe.wait_ge(head_factor, n - 1)
                        mm(B[n % 2][:, :], ones, HSQ[:, n % 8, :], start=True, stop=True).then_inc(head_sum_done, 1)
                pe.wait_ge(d_glog, l + 1)
                glog = sm2(0, 8)
                mm(B[5][:, 0:16], k(C_TRIU), sm(0), start=True, stop=True).then_inc(decay_sums, 1)
                rope([swq[:, 2 * j:2 * j + 2, :] for j in range(4)] + [kd[:, :, :]], [True] * 5, C_PERM1)
                pe.wait_ge(rope_added, cnt["rp"])
                pe.wait_ge(head_normed, 8 * l + 8)
                pe.wait_ge(silu_done, 12 * l + 12)
                pe.wait_ge(d_coef, l + 1)
                for g in range(4):
                    c, h0, b = g // 2, 4 * (g % 2), 3 * (g % 2)
                    tk = slice(c * P, c * P + P)
                    if g >= 2:
                        pe.wait_ge(d_rows, 4 * l + g - 1)
                    for j in range(4):
                        mm(B[b][:, j * P:(j + 1) * P], glog[:, c, h0 + j:h0 + j + 1].to_broadcast([P, P]), k(C_TRIU), start=True, stop=True)
                    for j in range(4):
                        mm(B[b + 1][:, j * P:(j + 1) * P], qkv[:, 8 + h0 + j, tk], qkv[:, h0 + j, tk], start=True, stop=True)
                    for j in range(4):
                        last = mm(B[b + 2][:, j * P:(j + 1) * P], qkv[:, 8 + h0 + j, tk], qkv[:, 8 + h0 + j, tk], start=True, stop=True)
                    last.then_inc(prep_done, 1)
                for s in range(LEVELS):
                    for g in range(4):
                        n = 4 * (LEVELS * l + s) + g
                        wn = 4 * ((LEVELS - 1) * l + s - 1) + g
                        pe.wait_ge(offdiag_ready, n + 1)
                        if s == 0 and g >= 2:
                            pe.wait_ge(y_updated, n - 1)
                        if s == 0 and g < 2:
                            pe.wait_ge(d_rows, 4 * l + 4)
                        if s == 1:
                            pe.wait_ge(y_updated, 4 * (LEVELS * l + 1))
                        if s > 1:
                            pe.wait_ge(y_updated, n - 3)
                        if s > 1 or (s == 1 and g >= 2):
                            pe.wait_ge(w_copied, wn - 1)
                        for j in range(4):
                            last = mm(B[g % 2][:, j * P:(j + 1) * P], LO[:, g, j, :], ident if s == 0 else Y[:, g, j, :], start=True, stop=True)
                        last.then_inc(winv_done, 1)
                    for g in range(4):
                        if s == 0:
                            continue
                        n = 4 * (LEVELS * l + s) + g
                        wn = 4 * ((LEVELS - 1) * l + s - 1) + g
                        pe.wait_ge(w_copied, wn + 1)
                        if s > 1 or g >= 2:
                            pe.wait_ge(y_updated, n - 1)
                        by, bt = B[2 + 2 * (g % 2)], B[3 + 2 * (g % 2)]
                        for j in range(4):
                            last = mm(by[:, j * P:(j + 1) * P], YT[:, g, j, :], W[:, g, j, :], start=True, stop=True)
                        if s < LEVELS - 1:
                            for j in range(4):
                                last = mm(bt[:, j * P:(j + 1) * P], W[:, g, j, :], YT[:, g, j, :], start=True, stop=True)
                        last.then_inc(yinv_done, 1)
                pe.wait_ge(y_updated, 4 * LEVELS * (l + 1))
                for g in range(4):
                    c, h0 = g // 2, 4 * (g % 2)
                    tk = slice(c * P, c * P + P)
                    if g >= 2:
                        pe.wait_ge(kv_ready, 4 * l + g - 1)
                    for j in range(4):
                        tr(B[2 * (g % 2)][:, j * P:(j + 1) * P], qkv[:, 8 + h0 + j, tk], ident)
                    for j in range(4):
                        last = tr(B[2 * (g % 2) + 1][:, j * P:(j + 1) * P], qkv[:, 16 + h0 + j, tk], ident)
                    last.then_inc(kv_transposed, 1)
                pe.wait_ge(kv_ready, 4 * l + 4)
                base = 12 * l
                for hh in range(2):
                    for j in range(4):
                        last = mm(B[hh][:, j * P:(j + 1) * P], Y[:, hh, j, :], VX[:, hh, j, :], start=True, stop=True)
                    last.then_inc(step_done, 1)
                for hh in range(2):
                    for j in range(4):
                        last = mm(B[2 + hh][:, j * P:(j + 1) * P], KX[:, 2 + hh, j, :], Y[:, 2 + hh, j, :], start=True, stop=True)
                    last.then_inc(step_done, 1)
                for hh in range(2):
                    pe.wait_ge(step_copied, base + hh + 1)
                    for j in range(4):
                        last = mm(B[4 + hh][:, j * P:(j + 1) * P], KX[:, hh, j, :], U[:, hh, j, :], start=True, stop=True)
                    last.then_inc(step_done, 1)
                for hh in range(2):
                    for j in range(4):
                        last = mm(B[hh][:, j * P:(j + 1) * P], U[:, hh, j, :], QM[:, hh, j, :], start=True, stop=True)
                    last.then_inc(step_done, 1)
                for hh in range(2):
                    pe.wait_ge(step_copied, base + 5 + hh)
                    for j in range(4):
                        mm(B[2 + hh][:, j * P:(j + 1) * P], Y[:, 2 + hh, j, :], VX[:, 2 + hh, j, :], start=True, stop=False)
                        last = mm(B[2 + hh][:, j * P:(j + 1) * P], WT[:, hh, j, :], S1[:, hh, j, :], start=False, stop=True)
                    last.then_inc(step_done, 1)
                for hh in range(2):
                    pe.wait_ge(step_copied, base + 9 + hh)
                    for j in range(4):
                        mm(B[4 + hh][:, j * P:(j + 1) * P], S1[:, hh, j, :], QD[:, hh, j, :], start=True, stop=False)
                        last = mm(B[4 + hh][:, j * P:(j + 1) * P], U[:, 2 + hh, j, :], QM[:, 2 + hh, j, :], start=False, stop=True)
                    last.then_inc(step_done, 1)
                for i in range(4):
                    pe.wait_ge(out_squared, 4 * l + i + 1)
                    if i >= 2:
                        pe.wait_ge(out_factor, 4 * l + i - 1)
                    mm(B[i % 2][:, :], ones, OSQ[:, i, :], start=True, stop=True).then_inc(osum_done, 1)
                pe.wait_ge(out_factor, 4 * l + 4)
                pe.wait_ge(in_copied, INC["swq", l, 3])
                attention(16, swq, lambda hh: hh // 8, lambda hh, tt: vtok[:, tt, 64 * (hh // 8):64 * (hh // 8) + 64])
                pe.wait_ge(out_normed, l + 1)
                pe.wait_ge(pair_copied, cnt["pv"] // 2)
                for i in range(4):
                    linear(("dno", l, i), oT)
                pe.wait_ge(pair_copied, cnt["pv"] // 2)
                for i in range(4):
                    linear(("swo", l, i), atT)
                pe.wait_ge(merged, 8 * l + 8)
                for i in range(4):
                    linear(("wo", l, i), mrg)
                sum_squares(2 * l + 1)
                ffn("ua", "ul", "ud", l, 2 * l + 1, l)

            for l in range(LAYERS):
                ni = 4 + 3 * l
                sum_squares(ni)
                ffn("g1", "u1", "d1", l, ni, 2 + 2 * l)
                sum_squares(ni + 1)
                special("s2", l, ni + 1)
                for kind, n in (("aq", 2), ("qi", 1), ("qk", 4)):
                    for i in range(n):
                        linear3((kind, l, i), h_high, h_low)
                for i in range(2):
                    w = arrive(("vm", l, i))
                    o = LV[R["vm", l, i] % 2]
                    token_major(lambda t: w[:, t, :], lambda tt: o[:, tt, :]).then_inc(chunk_multiplied, 1)
                for i in range(2):
                    linear3(("om", l, i), h_high, h_low)
                rope([swq[:, 0:2, :], swq[:, 2:4, :], swq[:, 4:6, :], kd[:, :, :]], [True, True, False, True], C_PERM2)
                pe.wait_ge(rope_added, cnt["rp"])
                for hh in range(4):
                    if hh >= 2:
                        pe.wait_ge(index_read, 4 * l + hh - 1)
                    b, lo = B[hh % 2], 64 * (hh % 2)
                    kk = kd[lo:lo + 64, 1, :]
                    mm(b[:, 0:P], swq[lo:lo + 64, 4 + hh // 2, 0:P], kk[:, 0:P], start=True, stop=True)
                    mm(b[:, P:3 * P], swq[lo:lo + 64, 4 + hh // 2, P:T], kk, start=True, stop=True).then_inc(index_done, 1)
                pe.wait_ge(m_gates, l + 1)
                nlf, gi = sm2(0, 4), sm2(1, 4)
                mm(B[2][:, 0:8], k(C_TRIU), sm(0, 8), start=True, stop=True)
                mm(B[2][:, 8:16], ones, sm(0, 8), start=True, stop=True).then_inc(m_sums, 1)
                for c in range(2):
                    for j in range(4):
                        o = B[3 + c][:, j * P:(j + 1) * P]
                        mm(o, gi[:, c, j:j + 1].to_broadcast([P, P]), ident, start=True, stop=False)
                        last = mm(o, nlf[:, c, j:j + 1].to_broadcast([P, P]), k(C_TRIU), start=False, stop=True)
                last.then_inc(m_rows, 1)
                pe.wait_ge(silu_done, 24 + 4 * l + 4)
                for j in range(4):
                    last = tr(B[5][:, j * P:(j + 1) * P], qkm[:, 4 + j, 0:P], ident)
                last.then_inc(m_keys, 1)
                pe.wait_ge(m_arc, l + 1)
                for c in range(2):
                    for j in range(4):
                        last = mm(B[3 + c][:, j * P:(j + 1) * P], qkm[:, 4 + j, c * P:(c + 1) * P], qkm[:, j, c * P:(c + 1) * P], start=True, stop=True)
                last.then_inc(m_scores, 1)
                pe.wait_ge(m_kx, l + 1)
                pe.wait_ge(m_columns, l + 1)
                pe.wait_ge(in_copied, INC["vm", l, 1])
                for j in range(4):
                    last = mm(B[2 if j < 2 else 5][:, (j % 2) * T:(j % 2) * T + 129], mKX[:, j, :], vaug[:, 0, j, 0:129], start=True, stop=True)
                last.then_inc(m_state, 1)
                pe.wait_ge(m_ca, l + 1)
                pe.wait_ge(index_read, 4 * l + 4)
                for c in range(2):
                    for j in range(4):
                        o = B[(3, 4, 0, 1)[2 * c + j // 2]][:, (j % 2) * T:(j % 2) * T + 129]
                        last = mm(o, mS[:, c, j, :], vaug[:, c, j, 0:129], start=True, stop=(c == 0))
                        if c == 1:
                            last = mm(o, mQD[:, j, :], mCA[:, j, 0:129], start=False, stop=True)
                last.then_inc(m_nums, 1)
                pe.wait_ge(m_h, l + 1)
                for c in range(2):
                    for j in range(4):
                        last = tr(B[2 if c == 0 else 5][:, j * P:(j + 1) * P], mH[:, c, j, :], ident)
                last.then_inc(m_turned, 1)
                pe.wait_ge(m_added, l + 1)
                pe.wait_ge(in_copied, INC["om", l, 1])
                attention(8, swq, lambda hh: 0, lambda hh, tt: vtok[:, tt, 0:64])
                pe.wait_ge(pair_copied, cnt["pv"] // 2)
                for i in range(4):
                    linear(("out", l, i), atT)
                sum_squares(ni + 2)
                ffn("g2", "u2", "d2", l, ni + 2, 3 + 2 * l)
            pe.wait_ge(x_done, total_x)
            for u in range(4):
                for j in range(4):
                    last = tr(B[u][:, j * P:(j + 1) * P], x[:, 4 * (u % 2) + j, (u // 2) * P:(u // 2) * P + P], ident)
                last.then_inc(final_transposed, 1)
        @block.vector
        def _(dve):
            v = nc.vector
            count = [0]

            def then(*ins):
                for i in ins:
                    i.then_inc(v_chain, 1)
                count[0] += len(ins)
                dve.wait_ge(v_chain, count[0])

            B5v = B[5][:, :].rearrange("p (c n) -> p c n", c=2)

            made = [0]

            def split(upto):
                while made[0] < min(upto, len(SPLIT)):
                    n = made[0]
                    q = Q[SPLIT[n]]
                    dve.wait_ge(chunk_rounded, n + 1)
                    raw = slot(q)[:, 0:2 * D].rearrange("p (t n) -> p t n", t=KT)
                    v.tensor_tensor(WL[n % 2][:, :, :], raw, WH[n % 2][:, :, :].bitcast(F32), ALU.subtract).then_inc(chunk_split, 1)
                    made[0] += 1

            def modulate(l, i):
                q = Q["ada", l, i]
                dve.wait_ge(w_landed[q % NS], landed[q])
                w = slot(q)[:, 0:2 * D].rearrange("p (t n) -> p t n", t=KT)
                dst = acc[:, 256 * i:256 * i + 256]
                then(v.tensor_scalar(dst, w[:, 0, :], ccol[:, 0:1], None, ALU.mult))
                for t in range(1, KT):
                    ins = v.scalar_tensor_tensor(out=dst, in0=w[:, t, :], scalar=ccol[:, t:t + 1], in1=dst, op0=ALU.mult, op1=ALU.add)
                    if t < KT - 1:
                        then(ins)
                    else:
                        ins.then_inc(chunk_modulated, 1)

            def scale(ni, cols, biased):
                dve.wait_ge(x_done, x_steps[ni][3])
                dve.wait_ge(norm_factor, ni + 1)
                for t in range(KT):
                    v.scalar_tensor_tensor(out=(tmp if biased else h)[:, t, :], in0=x[:, t, :], scalar=cols(t), in1=rinv[:, :],
                                               op0=ALU.mult, op1=ALU.mult).then_inc(h_scaled, 1)
                for t in range(KT):
                    dve.wait_ge(h_rounded, KT * ni + t + 1)
                    v.tensor_tensor(h_low[:, t, :], h[:, t, :], h_high[:, t, :].bitcast(F32), ALU.subtract).then_inc(norm_ready, 1)

            def conv(key, n, taps, cols, bias):
                dve.wait_ge(chunk_multiplied, M[key] + 1)
                if n >= 2:
                    dve.wait_ge(silu_done, n - 1)
                ps = LV[R[key] % 2]
                dst = CV[:, n % 2, :].rearrange("p (m t) -> p m t", m=2)
                causal_taps(ps, dst, taps, cols, bias, conv_done)

            def causal_taps(ps, dst, taps, cols, bias, signal):
                then(*[v.tensor_scalar(dst[:, m, :], ps[:, m, :], cols(taps - 1, m), bias(m) if bias else None,
                                       ALU.mult, ALU.add) if bias else
                       v.tensor_scalar(dst[:, m, :], ps[:, m, :], cols(taps - 1, m), None, ALU.mult) for m in range(2)])
                for s in range(1, taps):
                    ins = [v.scalar_tensor_tensor(out=dst[:, m, s:T], in0=ps[:, m, 0:T - s], scalar=cols(taps - 1 - s, m),
                                                  in1=dst[:, m, s:T], op0=ALU.mult, op1=ALU.add) for m in range(2)]
                    if s < taps - 1:
                        then(*ins)
                    else:
                        then(ins[0])
                        ins[1].then_inc(signal, 1)

            turned, factored, normed_n = [0], [0], [0]

            def rope(pieces, cos, sin):
                for j, (src, w, tiles) in enumerate(pieces):
                    if w is None:
                        continue
                    factored[0] += 1
                    dve.wait_ge(rope_factor, factored[0])
                    r = RRV[:, j, :].rearrange("p (m t) -> p m t", m=2)
                    v.scalar_tensor_tensor(out=src[:, 0:tiles, :], in0=src[:, 0:tiles, :], scalar=w, in1=r[:, 0:tiles, :],
                                               op0=ALU.mult, op1=ALU.mult).then_inc(rope_normed, 1)
                dve.wait_ge(rope_normed, factored[0])
                rt = rtmp.rearrange("p (m t) -> p m t", m=2)
                for src, _, _ in pieces:
                    n = turned[0]
                    dve.wait_ge(rope_turned, n + 1)
                    if n:
                        dve.wait_ge(rope_added, n)
                    then(v.tensor_tensor(rt, B[2 + n % 2][:, :].rearrange("p (m t) -> p m t", m=2), over(sin, 2), ALU.mult),
                         v.tensor_tensor(src, src, over(cos, 2), ALU.mult))
                    v.tensor_tensor(src, src, rt, ALU.add).then_inc(rope_added, 1)
                    turned[0] += 1

            scored, lots = [0], [0]

            def attention(nh, mask, sink):
                def masked(lot):
                    gl = lots[0] + lot
                    buf = gl % 2
                    if gl >= 2:
                        dve.wait_ge(probs_transposed, 4 * (gl - 1))
                    for h4 in range(4):
                        n = scored[0]
                        dve.wait_ge(scores_done, n + 1)
                        v.scalar_tensor_tensor(out=SP[:, buf, h4, :], in0=B[n % 3][:, 0:384], scalar=0.125, in1=mask,
                                                   op0=ALU.mult, op1=ALU.add).then_inc(rows_masked, 1)
                        scored[0] += 1
                    dve.wait_ge(rows_masked, scored[0])
                    nm = sm2(10 + buf, 4)
                    then(v.tensor_reduce(nm[:, 0, :], SP[:, buf, :, 0:P], AXX, ALU.max),
                         v.tensor_reduce(nm[:, 1, :], SP[:, buf, :, P:3 * P], AXX, ALU.max))
                    if sink is not None:
                        sk = over(sink[:, 4 * lot:4 * lot + 4], 2)
                        then(v.tensor_tensor(nm, nm, sk, ALU.max))
                    last = v.tensor_scalar(nm, nm, -1.0, None, ALU.mult)
                    if sink is not None:
                        then(last)
                        last = v.tensor_tensor(sm2(14 + buf, 4), nm, sk, ALU.add)
                    last.then_inc(rows_max, 1)

                def normalised(lot):
                    gl = lots[0] + lot
                    buf = gl % 2
                    dve.wait_ge(exp_done, gl + 1)
                    rs = sm(12 + buf, 8)
                    if sink is not None:
                        then(v.tensor_tensor(rs, rs, sm(14 + buf, 8), ALU.add))
                    then(v.reciprocal(rs, rs))
                    r = sm2(12 + buf, 4)
                    then(v.tensor_tensor(SP[:, buf, :, 0:P], SP[:, buf, :, 0:P], bcast(r[:, 0, :], P), ALU.mult))
                    v.tensor_tensor(SP[:, buf, :, P:3 * P], SP[:, buf, :, P:3 * P], bcast(r[:, 1, :], 2 * P), ALU.mult).then_inc(probs_ready, 1)

                n = nh // 4
                masked(0)
                for lot in range(n):
                    if lot + 1 < n:
                        masked(lot + 1)
                    normalised(lot)
                lots[0] += n

            def hidden(key, fi, i, act, ahead):
                dve.wait_ge(chunk_multiplied, M[key] + 1)
                if i >= 2:
                    dve.wait_ge(hidden_ready, FP * fi + i - 1)
                v.tensor_tensor(HT[:, i % 2, :], act, L[R[key] % 2][:, :], ALU.mult).then_inc(hid_whole, 1)
                split(ahead)
                dve.wait_ge(hid_rounded, FP * fi + i + 1)
                v.tensor_tensor(hidL[:, i % 3, :], HT[:, i % 2, :], hidH[:, i % 3, :].bitcast(F32), ALU.subtract).then_inc(hidden_ready, 1)

            def gated_ffn(ka, kb, kc, l, fi, name):
                for i in range(FP):
                    split(SI[ka, l, i] + 2)
                    split(SI[kb, l, i] + 2)
                    dve.wait_ge(ffn_act, FP * fi + i + 1)
                    hidden((kb, l, i), fi, i, FA[:, i % 2, :], SI[kb, l, i] + (3 if i else 2))
                split(SI[kc, l, FP - 1] + 2)
                dve.wait_ge(chunk_multiplied, M[kc, l, FP - 1] + 1)
                for m in range(4):
                    xx = x[:, 2 * m:2 * m + 2, :]
                    v.scalar_tensor_tensor(out=xx, in0=B[m][:, :].rearrange("p (m t) -> p m t", m=2), scalar=0.5, in1=xx,
                                               op0=ALU.mult, op1=ALU.add).then_inc(x_done, 1)

            dve.wait_ge(inputs_landed, 16 * N_IN)
            v.tensor_copy(posf[0:1, :], posi[:, :]).then_inc(start_v, 1)
            dve.wait_ge(start_transposed, 1)
            ins = []
            for n in range(8):
                r = V_ROWS[n % 3] if n < 6 else V_ROWS[3]
                ins.append(v.tensor_copy(vcol[:, n, 0:r], B[n // 4][:, (n % 4) * P:(n % 4) * P + r]))
            ins.append(v.tensor_copy(ccol[:, :], B[2][:, 0:KT]))
            ins.append(v.tensor_copy(heads[:, :], B[2][:, P:P + R_ALL]))
            ins.append(v.tensor_scalar(ta, B[2][:, T:2 * T], col(COL_INV), None, ALU.mult))
            then(*ins)
            v.tensor_scalar(tb_, ta, float(1 / (2 * np.pi)), 12582912.0, ALU.mult, ALU.add).then_inc(start_v, 1)
            dve.wait_ge(start_v, 2)
            then(v.tensor_scalar(tb_, tb_, 12582912.0, None, ALU.subtract))
            then(v.scalar_tensor_tensor(out=ta, in0=tb_, scalar=-6.28125, in1=ta, op0=ALU.mult, op1=ALU.add))
            then(v.scalar_tensor_tensor(out=ta, in0=tb_, scalar=-(2 * np.pi - 6.28125), in1=ta, op0=ALU.mult, op1=ALU.add))
            then(v.tensor_scalar(ta, ta, 3.1415925, -3.1415925, ALU.min, ALU.max))
            v.scalar_tensor_tensor(out=tc_, in0=ta, scalar=-1.0, in1=ta, op0=ALU.mult, op1=ALU.max).then_inc(start_v, 1)
            for u, b in enumerate((B[3], B[4], B[5], L[0])):
                dve.wait_ge(start_transposed, u + 2)
                v.tensor_copy(x[:, 2 * u:2 * u + 2, :], b[:, :].rearrange("p (m t) -> p m t", m=2)).then_inc(x_done, 1)
            dve.wait_ge(start_a, 1)
            then(v.tensor_scalar_add(modc[:, 0:KT], modc[:, 0:KT], 1.0), v.tensor_scalar(nea[:, :], nea[:, :], -1.0, None, ALU.mult))
            then(v.reciprocal(modc[:, 0:KT], modc[:, 0:KT]))
            v.tensor_tensor(ccol[:, :], ccol[:, :], modc[:, 0:KT], ALU.mult).then_inc(start_v, 1)
            dve.wait_ge(start_v, 4)

            for l in range(LAYERS):
                va = VT[0, l]
                if l == 0:
                    for i in range(24):
                        modulate(0, i)
                dve.wait_ge(mod_summed, l + 1)
                then(v.tensor_tensor(modc[:, :], B[5][:, 0:48], vcol[:, va, 0:48], ALU.add))
                then(v.scalar_tensor_tensor(out=scol[:, 0:8], in0=modc[:, 8:16], scalar=1.0, in1=vcol[:, va, 48:56], op0=ALU.add, op1=ALU.mult),
                     v.scalar_tensor_tensor(out=scol[:, 8:16], in0=modc[:, 32:40], scalar=1.0, in1=vcol[:, va, 56:64], op0=ALU.add, op1=ALU.mult))
                split(SI["qkv", l, 0] + 1)
                scale(2 * l, lambda t: scol[:, t:t + 1], True)
                dve.wait_ge(chunk_multiplied, M["s1", l, 0] + 1)
                then(v.tensor_tensor(sm2(1, 8), B5v[:, :, 128:136], over(heads[:, R_DTB + 8 * l:R_DTB + 8 * l + 8], 2), ALU.add))
                v.scalar_tensor_tensor(out=sm(2), in0=sm(1), scalar=-1.0, in1=sm(1), op0=ALU.mult, op1=ALU.min).then_inc(d_x, 1)
                vb = VT[1, l]
                for i in range(12):
                    split(SI["qkv", l, i] + 2)
                    conv(("qkv", l, i), 12 * l + i, 4, lambda tap, m: vcol[:, vb, 24 * tap + 2 * i + m:24 * tap + 2 * i + m + 1], None)
                dve.wait_ge(d_e, l + 1)
                then(v.scalar_tensor_tensor(out=sm(3), in0=sm(1), scalar=0.0, in1=sm(3), op0=ALU.max, op1=ALU.add),
                     v.tensor_scalar_add(sm(4), sm(4), 1.0))
                v.tensor_tensor(sm2(0, 8), sm2(3, 8), over(nea[:, 8 * l:8 * l + 8], 2), ALU.mult).then_inc(d_glog, 1)
                then(v.reciprocal(sm(4), sm(4)))
                split(SI["swq", l, 3] + 1)
                dve.wait_ge(decay_sums, l + 1)
                v.tensor_copy(sm(5), B[5][:, 0:16]).then_inc(d_gcc, 1)
                dve.wait_ge(d_egc, l + 1)
                v.scalar_tensor_tensor(out=sm(7), in0=sm(4), scalar=-1.0, in1=sm(6), op0=ALU.mult, op1=ALU.mult).then_inc(d_coef, 1)
                rope([(swq[:, 2 * j:2 * j + 2, :], vc(0, l, VA["swa_q_norm"]), 2) for j in range(4)]
                     + [(kd[:, :, :], vc(0, l, VA["swa_k_norm"]), 2)], cosr[:, :], sinr[:, :])
                dve.wait_ge(rope_added, turned[0])
                gcc, beta, nbe, kc = sm2(5, 8), sm2(4, 8), sm2(7, 8), sm(8, 8)
                f4 = lambda ap: ap.rearrange("p (a b) -> p a b", a=4)

                def exponents(g):
                    c, h0 = g // 2, 4 * (g % 2)
                    dve.wait_ge(prep_done, 4 * l + g + 1)
                    if g >= 2:
                        dve.wait_ge(d_exp, 4 * l + g - 1)
                    gb_ = f4(B[3 * (g % 2)][:, :])
                    t1, tu, tl = f4(T1[:, g % 2, :]), f4(TU[:, g % 2, :]), f4(TL[:, g % 2, :])
                    ins = [v.tensor_tensor(t1, gb_, bcast(gcc[:, c, h0:h0 + 4], P), ALU.subtract)]
                    if c == 0:
                        ins.append(v.tensor_tensor(kc[:, h0:h0 + 4], gb_[:, :, P - 1], gcc[:, 0, h0:h0 + 4], ALU.subtract))
                    then(*ins)
                    then(v.tensor_tensor(tu, t1, over(k(C_MU), 4), ALU.add))
                    v.tensor_tensor(tl, over(k(C_ML), 4), t1, ALU.subtract).then_inc(d_exponent, 1)

                def rows(g):
                    c, h0 = g // 2, 4 * (g % 2)
                    dve.wait_ge(d_exp, 4 * l + g + 1)
                    b = 3 * (g % 2)
                    then(v.tensor_tensor(QM[:, g, :, :], f4(B[b + 1][:, :]), f4(TU[:, g % 2, :]), ALU.mult),
                         v.tensor_tensor(LL[:, g, :, :], f4(B[b + 2][:, :]), bcast(beta[:, c, h0:h0 + 4], P), ALU.mult))
                    if c == 1:
                        qd = QD[:, g - 2, :, :]
                        then(v.tensor_tensor(qd, qd, qkv[:, h0:h0 + 4, P:T], ALU.mult))
                    v.tensor_tensor(LL[:, g, :, :], LL[:, g, :, :], f4(TL[:, g % 2, :]), ALU.mult).then_inc(d_rows, 1)

                for g in range(5):
                    if g < 4:
                        exponents(g)
                    if g >= 1:
                        rows(g - 1)
                for s in range(LEVELS):
                    for g in range(4):
                        n = 4 * (LEVELS * l + s) + g
                        if s == 0:
                            dve.wait_ge(winv_done, n + 1)
                            then(v.tensor_tensor(Y[:, g, :, :], over(ident, 4), f4(B[g % 2][:, :]), ALU.subtract))
                            v.tensor_tensor(YT[:, g, :, :], over(ident, 4), LO[:, g, :, :], ALU.subtract).then_inc(y_updated, 1)
                            continue
                        dve.wait_ge(yinv_done, 4 * ((LEVELS - 1) * l + s - 1) + g + 1)
                        ins = [v.tensor_tensor(Y[:, g, :, :], Y[:, g, :, :], f4(B[2 + 2 * (g % 2)][:, :]), ALU.subtract)]
                        if s < LEVELS - 1:
                            then(*ins)
                            ins = [v.tensor_tensor(YT[:, g, :, :], YT[:, g, :, :], f4(B[3 + 2 * (g % 2)][:, :]), ALU.subtract)]
                        ins[0].then_inc(y_updated, 1)
                for g in range(4):
                    c, h0 = g // 2, 4 * (g % 2)
                    dve.wait_ge(kv_transposed, 4 * l + g + 1)
                    kcf = kc[:, h0:h0 + 4] if c == 0 else nbe[:, 1, h0:h0 + 4]
                    then(v.tensor_tensor(KX[:, g, :, :], f4(B[2 * (g % 2)][:, :]), bcast(kcf, P), ALU.mult))
                    v.tensor_tensor(VX[:, g, :, :], f4(B[2 * (g % 2) + 1][:, :]), bcast(beta[:, c, h0:h0 + 4], P), ALU.mult).then_inc(kv_ready, 1)
                places = [(U[:, 0], 0), (U[:, 1], 1), (WT[:, 0], 2), (WT[:, 1], 3), (S1[:, 0], 4), (S1[:, 1], 5), (oT[:, 0:4, 0:P], 0),
                          (oT[:, 4:8, 0:P], 1), (U[:, 2], 2), (U[:, 3], 3), (oT[:, 0:4, P:T], 4), (oT[:, 4:8, P:T], 5)]
                for n, (dst, b) in enumerate(places):
                    dve.wait_ge(step_done, 12 * l + n + 1)
                    v.tensor_copy(dst, f4(B[b][:, :])).then_inc(step_copied, 1)
                for i in range(4):
                    dve.wait_ge(out_factor, 4 * l + i + 1)
                    o = oT[:, 2 * i:2 * i + 2, :]
                    then(v.scalar_tensor_tensor(out=o, in0=o, scalar=vc(0, l, VA["dn_norm"]), in1=ORV[:, i, :].rearrange("p (m t) -> p m t", m=2),
                                                op0=ALU.mult, op1=ALU.mult))
                    ins = v.tensor_tensor(o, o, zbuf[:, 2 * i:2 * i + 2, :], ALU.mult)
                    if i < 3:
                        then(ins)
                    else:
                        ins.then_inc(out_normed, 1)
                attention(16, K[:, C_SWA:C_SWA + 384], heads[:, R_SINK + 16 * l:R_SINK + 16 * l + 16])
                for i in range(4):
                    key = ("dno", l, i)
                    dve.wait_ge(chunk_multiplied, M[key] + 1)
                    v.tensor_tensor(mrg[:, 2 * i:2 * i + 2, :], LV[R[key] % 2], gab[:, 2 * i:2 * i + 2, :], ALU.mult).then_inc(merged, 1)
                for i in range(4):
                    key = ("swo", l, i)
                    dve.wait_ge(chunk_multiplied, M[key] + 1)
                    y2 = yb[:, 2 * i:2 * i + 2, :]
                    then(v.tensor_tensor(y2, LV[R[key] % 2], gbb[:, 2 * i:2 * i + 2, :], ALU.mult))
                    v.tensor_tensor(mrg[:, 2 * i:2 * i + 2, :], mrg[:, 2 * i:2 * i + 2, :], y2, ALU.add).then_inc(merged, 1)
                for i in range(4):
                    key = ("wo", l, i)
                    dve.wait_ge(chunk_multiplied, M[key] + 1)
                    for m in range(2):
                        t = 2 * i + m
                        v.scalar_tensor_tensor(out=x[:, t, :], in0=LV[R[key] % 2][:, m, :], scalar=modc[:, 16 + t:17 + t],
                                                   in1=x[:, t, :], op0=ALU.mult, op1=ALU.add).then_inc(x_done, 1)
                split(SI["ua", l, 0] + 2)
                scale(2 * l + 1, lambda t: scol[:, 8 + t:9 + t], True)
                vf = VT[2, l]
                for i in range(FP + 1):
                    if l == 0:
                        for m in range(2):
                            if i >= 1:
                                modulate(1, 2 * i - 2 + m)
                    if i == FP:
                        break
                    split(SI["ul", l, i] + 2)
                    dve.wait_ge(chunk_multiplied, M["ua", l, i] + 1)
                    if i >= 2:
                        dve.wait_ge(hidden_ready, FP * l + i - 1)
                    fa, fb = FA[:, i % 2, :], FB[:, i % 2, :]
                    causal_taps(LV[R["ua", l, i] % 2], fb.rearrange("p (m t) -> p m t", m=2), 3,
                                lambda tap, m: vcol[:, vf, FT * tap + 2 * i + m:FT * tap + 2 * i + m + 1],
                                lambda m: vcol[:, vf, 66 + 2 * i + m:67 + 2 * i + m], fconv_done)
                    if l and i:
                        split(SI["ul", l, i] + 3)
                    dve.wait_ge(ffn_act, FP * l + i + 1)
                    hidden(("ul", l, i), l, i, fa, SI["ul", l, i] + (3 if i and l else 2))
                split(SI["ud", l, FP - 1] + 1)
                if l == 0:
                    for m in range(2):
                        modulate(1, 2 * FP + m)
                dve.wait_ge(chunk_multiplied, M["ud", l, FP - 1] + 1)
                for t in range(KT):
                    v.scalar_tensor_tensor(out=x[:, t, :], in0=B[t // 2][:, (t % 2) * T:(t % 2) * T + T], scalar=modc[:, 40 + t:41 + t],
                                               in1=x[:, t, :], op0=ALU.mult, op1=ALU.add).then_inc(x_done, 1)

            for l in range(LAYERS):
                ni, vd = 4 + 3 * l, VT[3, l]
                scale(ni, lambda t: vcol[:, vd, t:t + 1], False)
                gated_ffn("g1", "u1", "d1", l, 2 + 2 * l, "ffn1")
                scale(ni + 1, lambda t: vcol[:, vd, 8 + t:9 + t], False)
                dve.wait_ge(chunk_multiplied, M["s2", l, 0] + 1)
                gb0 = heads[:, R_GB + 8 * l:R_GB + 8 * l + 8]
                then(v.tensor_tensor(sm2(1, 4), B5v[:, :, 68:72], over(gb0[:, 0:4], 2), ALU.add),
                     v.tensor_tensor(sm2(2, 4), B5v[:, :, 72:76], over(gb0[:, 4:8], 2), ALU.add),
                     v.tensor_copy(sm2(5, 4), B5v[:, :, 64:68]),
                     v.memset(vaug[:, :, :, 128:129], 1.0))
                v.scalar_tensor_tensor(out=sm(3, 8), in0=sm(2, 8), scalar=-1.0, in1=sm(2, 8), op0=ALU.mult, op1=ALU.min).then_inc(m_pre, 1)
                split(SI["qk", l, 0] + 1)
                for i in range(4):
                    split(min(SI["qk", l, i], SI["om", l, 1] - 1) + 2)
                    conv(("qk", l, i), 24 + 4 * l + i, 4, lambda tap, m: vcol[:, vd, 24 + 8 * tap + 2 * i + m:25 + 8 * tap + 2 * i + m],
                         lambda m: vcol[:, vd, 56 + 2 * i + m:57 + 2 * i + m])
                split(SI["om", l, 1] + 1)
                dve.wait_ge(m_l, l + 1)
                then(v.tensor_scalar(sm(6, 8), sm(2, 8), -1.0, 0.0, ALU.mult, ALU.max))
                v.tensor_tensor(sm(0, 8), sm(6, 8), sm(4, 8), ALU.add).then_inc(m_gates, 1)
                dve.wait_ge(in_copied, INC["om", l, 1])
                dve.wait_ge(silu_done, 24 + 4 * l + 4)
                rope([(swq[:, 0:2, :], vc(3, l, 64), 2), (swq[:, 2:4, :], vc(3, l, 64), 2), (swq[:, 4:6, :], None, 0),
                      (kd[:, :, :], vc(3, l, 65), 1)], K[:, C_COS2:C_COS2 + T], K[:, C_SIN2:C_SIN2 + T])
                wi = sm2(5, 4)
                for hh in range(4):
                    dve.wait_ge(index_done, 4 * l + hh + 1)
                    b = B[hh % 2]
                    dst = IX if hh == 0 else IT[:, hh % 2, :]
                    then(v.tensor_scalar(dst[:, 0:P], b[:, 0:P], 0.0, wi[:, 0, hh:hh + 1], ALU.max, ALU.mult))
                    v.tensor_scalar(dst[:, P:3 * P], b[:, P:3 * P], 0.0, wi[:, 1, hh:hh + 1], ALU.max, ALU.mult).then_inc(index_read, 1)
                    dve.wait_ge(index_read, 4 * l + hh + 1)
                    if hh:
                        then(v.tensor_tensor(IX, IX, dst, ALU.add))
                dve.wait_ge(m_sums, l + 1)
                nb, tot, acol, mc, m1, ca, em = sm2(19, 4), sm2(20, 4), sm2(18, 4), sm2(21, 4), sm(22, 4), sm(23, 4), sm(24, 8)
                then(v.tensor_copy(sm(19, 8), B[2][:, 0:8]), v.tensor_copy(sm(20, 8), B[2][:, 8:16]))
                v.tensor_tensor(sm(18, 8), sm(1, 8), sm(19, 8), ALU.add).then_inc(m_columns, 1)
                dve.wait_ge(m_columns, l + 1)
                dve.wait_ge(m_arc, l + 1)
                for c in range(2):
                    then(*[v.tensor_tensor_scan(mMR[:, c, j, :], mAR[:, c, j, :], mAR[:, c, j, :], m1[:, j:j + 1] if c else 0.0, ALU.max, ALU.max)
                           for j in range(4)])
                    if c == 0:
                        then(v.tensor_tensor(m1, mMR[:, 0, :, P - 1], tot[:, 0, :], ALU.subtract))
                f8 = lambda ap: ap.rearrange("p c h t -> p (c h) t")
                then(v.tensor_tensor(f8(mX), f8(mMR), over(ident, 8), ALU.mult),
                     v.tensor_tensor(f8(mT), over(k(C_MU), 8), f8(mMR), ALU.subtract),
                     v.tensor_tensor(ca, acol[:, 0, :], mMR[:, 0, :, P - 1], ALU.subtract))
                then(v.tensor_reduce(sm(21, 8), f8(mX), AXX, ALU.add))
                v.tensor_tensor(em, sm(19, 8), sm(21, 8), ALU.subtract).then_inc(m_masked, 1)
                dve.wait_ge(m_expd, l + 1)
                dve.wait_ge(m_keys, l + 1)
                v.scalar_tensor_tensor(out=mKX, in0=f4(B[5][:, :]), scalar=float(P) ** -0.5, in1=bcast(ca, P), op0=ALU.mult, op1=ALU.mult).then_inc(m_kx, 1)
                dve.wait_ge(m_scores, l + 1)
                then(*[v.scalar_tensor_tensor(out=mS[:, c, :, :], in0=f4(B[3 + c][:, :]), scalar=float(P) ** -0.5, in1=mT[:, c, :, :],
                                              op0=ALU.mult, op1=ALU.mult) for c in range(2)],
                     v.tensor_tensor(mQD, mQD, qkm[:, 0:4, P:T], ALU.mult))
                dve.wait_ge(m_state, l + 1)
                two = lambda b: b[:, :].rearrange("p (m t) -> p m t", m=2)
                then(v.tensor_copy(mCA[:, 0:2, 0:129], two(B[2])[:, :, 0:129]))
                v.tensor_copy(mCA[:, 2:4, 0:129], two(B[5])[:, :, 0:129]).then_inc(m_ca, 1)
                dve.wait_ge(m_nums, l + 1)
                den = sm(25, 8)
                nums = (B[3], B[4], B[0], B[1])
                then(*[v.tensor_copy(den[:, 2 * n:2 * n + 2], two(b)[:, :, 128]) for n, b in enumerate(nums)])
                then(v.tensor_scalar(sm(26, 8), den, -1.0, None, ALU.mult))
                then(v.tensor_tensor(den, den, sm(26, 8), ALU.max))
                then(v.tensor_tensor(den, den, em, ALU.max))
                then(v.reciprocal(den, den))
                then(*[v.tensor_tensor(f8(mH)[:, 2 * n:2 * n + 2, :], two(b)[:, :, 0:P], bcast(den[:, 2 * n:2 * n + 2], P), ALU.mult)
                       for n, b in enumerate(nums)])
                then(v.tensor_tensor(f8(mX), f8(mH), f8(mH), ALU.mult))
                v.tensor_reduce(sm(27, 8), f8(mX), AXX, ALU.add).then_inc(m_w, 1)
                dve.wait_ge(m_factor, l + 1)
                v.tensor_tensor(f8(mH), f8(mH), bcast(sm(27, 8), P), ALU.mult).then_inc(m_h, 1)
                then(v.tensor_tensor(IW, IX, K[:, C_CAUS:C_CAUS + 384], ALU.add))
                best = small[:, 16 * 28:16 * 28 + 16]
                for _ in range(TOPK // 8):
                    then(v.max(out=best[:, 0:8], in_=IW[:, 0:P]), v.max(out=best[:, 8:16], in_=IW[:, P:3 * P]))
                    then(v.match_replace(out=IW[:, 0:P], in_to_replace=best[:, 0:8], in_values=IW[:, 0:P], imm_value=-3e38),
                         v.match_replace(out=IW[:, P:3 * P], in_to_replace=best[:, 8:16], in_values=IW[:, P:3 * P], imm_value=-3e38))
                then(v.tensor_scalar(IM, IW, -2e38, NEG, ALU.is_gt, ALU.mult))
                then(v.tensor_tensor(IM, IM, K[:, C_CAUS:C_CAUS + 384], ALU.add))
                dve.wait_ge(m_turned, l + 1)
                for c in range(2):
                    for j in range(4):
                        ins = v.scalar_tensor_tensor(out=atT[:, 4 + j, c * P:(c + 1) * P], in0=B[2 if c == 0 else 5][:, j * P:(j + 1) * P],
                                                     scalar=vc(3, l, 66 + j), in1=gab[:, j, c * P:(c + 1) * P], op0=ALU.mult, op1=ALU.mult)
                        if (c, j) == (1, 3):
                            ins.then_inc(m_added, 1)
                        else:
                            then(ins)
                attention(8, IM, None)
                for i in range(4):
                    key = ("out", l, i)
                    dve.wait_ge(chunk_multiplied, M[key] + 1)
                    xx = x[:, 2 * i:2 * i + 2, :]
                    v.tensor_tensor(xx, xx, LV[R[key] % 2], ALU.add).then_inc(x_done, 1)
                split(SI["g2", l, 0] + 2)
                scale(ni + 2, lambda t: vcol[:, vd, 16 + t:17 + t], False)
                gated_ffn("g2", "u2", "d2", l, 3 + 2 * l, "ffn2")
            for u in range(4):
                dve.wait_ge(final_transposed, u + 1)
                v.tensor_copy(xin2[:, u // 2, 512 * (u % 2):512 * (u % 2) + 512], B[u][:, :]).then_inc(final_copied, 1)

        @block.scalar
        def _(act):
            a_ = nc.scalar.activation
            count = [0]

            def then(*ins):
                for i in ins:
                    i.then_inc(a_chain, 1)
                count[0] += len(ins)
                act.wait_ge(a_chain, count[0])

            def rsqrt(dst, src, scale, bias, name):
                then(a_(dst, src, ACT.Ln, bias=col(COL_EPS), scale=scale))
                a_(dst, dst, ACT.Exp, bias=bias, scale=-0.5).then_inc(name, 1)

            made = [0]

            def split(upto):
                while made[0] < min(upto, len(SPLIT)):
                    n = made[0]
                    q = Q[SPLIT[n]]
                    act.wait_ge(w_landed[q % NS], landed[q])
                    if n >= 2:
                        act.wait_ge(chunk_multiplied, M[SPLIT[n - 2]] + 1)
                    a_(WH[n % 2][:, :, :], slot(q)[:, 0:2 * D].rearrange("p (t n) -> p t n", t=KT), ACT.Copy).then_inc(chunk_rounded, 1)
                    made[0] += 1

            def norm(ni, shift, ahead=0):
                nc.scalar.preload_act_table_set("natural_log_exp_and_others")
                for u in range(4):
                    act.wait_ge(x_done, x_steps[ni][u])
                    a_(tmp[:, 2 * u:2 * u + 2, :], x[:, 2 * u:2 * u + 2, :], ACT.Square).then_inc(squares_ready, 1)
                split(ahead)
                act.wait_ge(norm_sum, ni + 1)
                rsqrt(rinv[:, :], B[4][:, 0:T], 1.0 / D, 0.0, norm_factor)
                for t in range(KT):
                    act.wait_ge(h_scaled, KT * ni + t + 1)
                    if shift is None:
                        a_(h_high[:, t, :], h[:, t, :], ACT.Copy).then_inc(h_rounded, 1)
                    else:
                        bias = modc[:, shift + t:shift + t + 1]
                        then(a_(h[:, t, :], tmp[:, t, :], ACT.Identity, bias=bias, scale=1.0))
                        a_(h_high[:, t, :], tmp[:, t, :], ACT.Identity, bias=bias, scale=1.0).then_inc(h_rounded, 1)

            def silu_of_conv(n, dst):
                act.wait_ge(conv_done, n + 1)
                a_(dst, CV[:, n % 2, :].rearrange("p (m t) -> p m t", m=2), ACT.Silu).then_inc(silu_done, 1)

            sums = [0]

            def rope(normed):
                for j, yes in enumerate(normed):
                    if yes:
                        n = sums[0]
                        act.wait_ge(rope_sum, n + 1)
                        rsqrt(RRV[:, j, :], B[n % 2][:, :], 1.0 / 64, 0.0, rope_factor)
                        sums[0] += 1

            lots, turned, pairs = [0], [0], [0]

            def attention(nh, sink):
                def exps(lot):
                    gl = lots[0] + lot
                    buf = gl % 2
                    act.wait_ge(rows_max, gl + 1)
                    nm, rs = sm2(10 + buf, 4), sm2(12 + buf, 4)
                    for b in range(2):
                        for h4 in range(4):
                            s = SP[:, buf, h4, 0:P] if b == 0 else SP[:, buf, h4, P:3 * P]
                            ins = a_(s, s, ACT.Exp, bias=nm[:, b, h4:h4 + 1], scale=1.0, accum_out=rs[:, b, h4:h4 + 1])
                            if (b, h4) == (1, 3) and not sink:
                                ins.then_inc(exp_done, 1)
                            else:
                                then(ins)
                    if sink:
                        a_(sm(14 + buf, 8), sm(14 + buf, 8), ACT.Exp).then_inc(exp_done, 1)

                def copies():
                    for _ in range(4):
                        n = turned[0]
                        act.wait_ge(probs_transposed, n + 1)
                        if n >= 2:
                            act.wait_ge(head_weighed, n - 1)
                        a_(PT[:, n % 2, :], B[3 + n % 2][:, 0:384], ACT.Copy).then_inc(probs_copied, 1)
                        turned[0] += 1
                        if turned[0] % 2 == 0 and turned[0] >= 2:
                            pair = pairs[0]
                            act.wait_ge(head_weighed, 2 * pair + 2)
                            a_(atT[:, pair % (nh // 2), :], L[pair % 2][:, 0:T], ACT.Copy).then_inc(pair_copied, 1)
                            pairs[0] += 1

                n = nh // 4
                exps(0)
                for lot in range(n):
                    if lot + 1 < n:
                        exps(lot + 1)
                    copies()
                lots[0] += n

            def round_hidden(kb, kc, l, fi, i):
                split(SI[kb, l, i] + (3 if i and (kb != "ul" or l) else 2))
                act.wait_ge(hid_whole, FP * fi + i + 1)
                if i >= 3:
                    act.wait_ge(chunk_multiplied, M[kc, l, i - 3] + 1)
                a_(hidH[:, i % 3, :], HT[:, i % 2, :], ACT.Copy).then_inc(hid_rounded, 1)

            def silu_of_gate(key, fi, i):
                split(SI[key] + 3)
                act.wait_ge(chunk_multiplied, M[key] + 1)
                if i >= 2:
                    act.wait_ge(hidden_ready, FP * fi + i - 1)
                a_(FA[:, i % 2, :], L[R[key] % 2][:, :], ACT.Silu).then_inc(ffn_act, 1)

            act.wait_ge(start_v, 2)
            then(a_(modc[:, 0:KT], ccol[:, :], ACT.Exp, scale=-1.0))
            a_(nea[:, :], heads[:, R_ALOG:R_ALOG + 16], ACT.Exp).then_inc(start_a, 1)
            act.wait_ge(start_v, 3)
            then(a_(sinr[:, :], ta, ACT.Sin))
            a_(cosr[:, :], tc_, ACT.Sin, bias=col(COL_HPI), scale=-1.0).then_inc(start_a, 1)

            for l in range(LAYERS):
                split(SI["qkv", l, 0] + 1)
                norm(2 * l, 0)
                act.wait_ge(chunk_multiplied, M["s1", l, 0] + 1)
                act.wait_ge(d_x, l + 1)
                then(a_(vtok[:, :, :], B[5][:, :].rearrange("p (c n) -> p c n", c=2)[:, :, 0:P], ACT.Copy),
                     a_(sm2(4, 8), B[5][:, :].rearrange("p (c n) -> p c n", c=2)[:, :, 136:144], ACT.Exp, scale=-1.0),
                     a_(sm(3), sm(2), ACT.Exp))
                a_(kd[:, :, :], LV[R["s1", l, 0] % 2], ACT.Copy).then_inc(in_copied, 1)
                a_(sm(3), sm(3), ACT.Ln, bias=col(COL_ONE), scale=1.0).then_inc(d_e, 1)
                for i in range(12):
                    split(SI["qkv", l, i] + 2)
                    silu_of_conv(12 * l + i, qkv[:, 2 * i:2 * i + 2, :])
                for kind, buf, func in (("z", zbuf, ACT.Silu), ("ga", gab, ACT.Sigmoid), ("gb", gbb, ACT.Sigmoid)):
                    for i in range(4):
                        split(SI[kind, l, i] + 2)
                        act.wait_ge(chunk_multiplied, M[kind, l, i] + 1)
                        a_(buf[:, 2 * i:2 * i + 2, :], LV[R[kind, l, i] % 2], func).then_inc(in_copied, 1)
                nc.scalar.preload_act_table_set("natural_log_exp_and_others")
                for i in range(4):
                    split(min(SI["swq", l, i] + 2, SI["swq", l, 3] + 1))
                    act.wait_ge(chunk_multiplied, M["swq", l, i] + 1)
                    a_(swq[:, 2 * i:2 * i + 2, :], LV[R["swq", l, i] % 2], ACT.Copy).then_inc(in_copied, 1)
                    for n in (8 * l + 2 * i, 8 * l + 2 * i + 1):
                        act.wait_ge(head_sum_done, n + 1)
                        if n >= 2:
                            act.wait_ge(head_normed, n - 1)
                        rsqrt(RV[:, n % 2, :], B[n % 2][:, :], 1.0, col(COL_QS) if n % 8 < 4 else 0.0, head_factor)
                act.wait_ge(d_gcc, l + 1)
                a_(sm(6), sm(5), ACT.Exp).then_inc(d_egc, 1)
                rope([True] * 5)
                for g in range(4):
                    act.wait_ge(d_exponent, 4 * l + g + 1)
                    tu, tl = TU[:, g % 2, :], TL[:, g % 2, :]
                    then(a_(tu, tu, ACT.Exp))
                    if g < 2:
                        kcs = sm(8, 8)[:, 4 * g:4 * g + 4]
                        then(a_(kcs, kcs, ACT.Exp))
                    else:
                        then(a_(QD[:, g - 2, :, :], B[3 * (g % 2)][:, :].rearrange("p (a b) -> p a b", a=4), ACT.Exp))
                    a_(tl, tl, ACT.Exp).then_inc(d_exp, 1)
                for s in range(1, LEVELS):
                    for g in range(4):
                        n = 4 * (LEVELS * l + s) + g
                        act.wait_ge(winv_done, n + 1)
                        if s >= 2:
                            act.wait_ge(yinv_done, 4 * ((LEVELS - 1) * l + s - 1) + g - 3)
                        a_(W[:, g, :, :], B[g % 2][:, :].rearrange("p (a b) -> p a b", a=4), ACT.Copy).then_inc(w_copied, 1)
                for i in range(4):
                    act.wait_ge(osum_done, 4 * l + i + 1)
                    rsqrt(ORV[:, i, :], B[i % 2][:, :], 1.0 / P, 0.0, out_factor)
                attention(16, True)
                norm(2 * l + 1, 24, ahead=SI["ua", l, 0] + 2)
                for i in range(FP):
                    split(SI["ul", l, i] + (3 if i and l else 2))
                    act.wait_ge(fconv_done, FP * l + i + 1)
                    if i >= 2:
                        act.wait_ge(hidden_ready, FP * l + i - 1)
                    a_(FA[:, i % 2, :], FB[:, i % 2, :], ACT.Silu).then_inc(ffn_act, 1)
                    round_hidden("ul", "ud", l, l, i)
                split(SI["ud", l, FP - 1] + 2)

            for l in range(LAYERS):
                ni = 4 + 3 * l
                norm(ni, None)
                for i in range(FP):
                    silu_of_gate(("g1", l, i), 2 + 2 * l, i)
                    round_hidden("u1", "d1", l, 2 + 2 * l, i)
                split(SI["d1", l, FP - 1] + 2)
                norm(ni + 1, None)
                act.wait_ge(chunk_multiplied, M["s2", l, 0] + 1)
                act.wait_ge(m_pre, l + 1)
                then(a_(vtok[:, :, 0:64], B[5][:, :].rearrange("p (c n) -> p c n", c=2)[:, :, 0:64], ACT.Copy),
                     a_(sm(4, 8), sm(3, 8), ACT.Exp))
                a_(kd[:, :, :], LV[R["s2", l, 0] % 2], ACT.Copy).then_inc(in_copied, 1)
                a_(sm(4, 8), sm(4, 8), ACT.Ln, bias=col(COL_ONE), scale=1.0).then_inc(m_l, 1)
                for kind, n, t0 in (("aq", 2, 0), ("qi", 1, 4)):
                    for i in range(n):
                        split(SI[kind, l, i] + 2)
                        act.wait_ge(chunk_multiplied, M[kind, l, i] + 1)
                        a_(swq[:, t0 + 2 * i:t0 + 2 * i + 2, :], LV[R[kind, l, i] % 2], ACT.Copy).then_inc(in_copied, 1)
                for i in range(4):
                    split(SI["qk", l, i] + 2)
                    silu_of_conv(24 + 4 * l + i, qkm[:, 2 * i:2 * i + 2, :])
                for i in range(2):
                    key = ("vm", l, i)
                    act.wait_ge(chunk_multiplied, M[key] + 1)
                    src = LV[R[key] % 2].rearrange("p c (h e) -> p c h e", h=2)
                    then(a_(vaug[:, 0, 2 * i:2 * i + 2, 0:P], src[:, 0], ACT.Copy))
                    a_(vaug[:, 1, 2 * i:2 * i + 2, 0:P], src[:, 1], ACT.Copy).then_inc(in_copied, 1)
                for i in range(2):
                    key = ("om", l, i)
                    split(SI["om", l, 1] + 1)
                    act.wait_ge(chunk_multiplied, M[key] + 1)
                    a_(gab[:, 2 * i:2 * i + 2, :], LV[R[key] % 2], ACT.Sigmoid).then_inc(in_copied, 1)
                nc.scalar.preload_act_table_set("natural_log_exp_and_others")
                rope([True, True, False, True])
                act.wait_ge(m_rows, l + 1)
                then(a_(mAR[:, 0, :, :], B[3][:, :].rearrange("p (a b) -> p a b", a=4), ACT.Copy))
                a_(mAR[:, 1, :, :], B[4][:, :].rearrange("p (a b) -> p a b", a=4), ACT.Copy).then_inc(m_arc, 1)
                act.wait_ge(m_masked, l + 1)
                acol, m1 = sm2(18, 4), sm(22, 4)
                then(*[a_(mT[:, c, j, :], mT[:, c, j, :], ACT.Exp, bias=acol[:, c, j:j + 1], scale=1.0) for c in range(2) for j in range(4)],
                     *[a_(mQD[:, j, :], mMR[:, 1, j, :], ACT.Exp, bias=m1[:, j:j + 1], scale=-1.0) for j in range(4)],
                     a_(sm(23, 4), sm(23, 4), ACT.Exp))
                a_(sm(24, 8), sm(24, 8), ACT.Exp).then_inc(m_expd, 1)
                act.wait_ge(m_w, l + 1)
                rsqrt(sm(27, 8), sm(27, 8), 1.0 / P, 0.0, m_factor)
                attention(8, False)
                norm(ni + 2, None, ahead=SI["g2", l, 0] + 2)
                for i in range(FP):
                    silu_of_gate(("g2", l, i), 3 + 2 * l, i)
                    round_hidden("u2", "d2", l, 3 + 2 * l, i)
                split(SI["d2", l, FP - 1] + 2)

        @block.gpsimd
        def _(pool):
            g_ = nc.gpsimd

            def rope_squares(pieces):
                for j, src, n in pieces:
                    pool.wait_ge(in_copied, n)
                    g_.tensor_tensor(RSQ[:, j, :].rearrange("p (m t) -> p m t", m=2), src, src, ALU.mult).then_inc(rope_squared, 1)

            for l in range(LAYERS):
                for i in range(16):
                    if i < 8:
                        n = 8 * l + i
                        pool.wait_ge(silu_done, 12 * l + i + 1)
                        qq = qkv[:, 2 * i:2 * i + 2, :]
                        g_.tensor_tensor(HSQ[:, i, :].rearrange("p (m t) -> p m t", m=2), qq, qq, ALU.mult).then_inc(head_squared, 1)
                    else:
                        n = 8 * l + i - 8
                        pool.wait_ge(head_factor, n + 1)
                        qq = qkv[:, 2 * i - 16:2 * i - 14, :]
                        g_.tensor_tensor(qq, qq, RV[:, n % 2, :].rearrange("p (m t) -> p m t", m=2), ALU.mult).then_inc(head_normed, 1)
                pool.wait_ge(chunk_multiplied, M["swq", l, 3] + 1)
                rope_squares([(j, swq[:, 2 * j:2 * j + 2, :], INC["swq", l, j]) for j in range(4)] + [(4, kd[:, :, :], INC["s1", l, 0])])
                for s in range(LEVELS):
                    for g in range(4):
                        if s == 0:
                            pool.wait_ge(d_rows, 4 * l + g + 1)
                        else:
                            pool.wait_ge(winv_done, 4 * (LEVELS * l + s - 1) + g + 1)
                        if s == 1:
                            pool.wait_ge(y_updated, 4 * LEVELS * l + g + 1)
                        g_.tensor_tensor(LO[:, g, :, :], LL[:, g, :, :], over(k(C_LV + s * P), 4), ALU.mult).then_inc(offdiag_ready, 1)
                pool.wait_ge(step_copied, 12 * l + 12)
                for i in range(4):
                    o = oT[:, 2 * i:2 * i + 2, :]
                    g_.tensor_tensor(OSQ[:, i, :].rearrange("p (m t) -> p m t", m=2), o, o, ALU.mult).then_inc(out_squared, 1)
            for l in range(LAYERS):
                pool.wait_ge(chunk_multiplied, M["om", l, 1] + 1)
                rope_squares([(0, swq[:, 0:2, :], INC["aq", l, 0]), (1, swq[:, 2:4, :], INC["aq", l, 1]), (3, kd[:, :, :], INC["s2", l, 0])])


def kernel(**inputs):
    import concourse.bacc as bacc
    from concourse.bass_utils import run_bass_kernel_spmd

    nc = bacc.Bacc("TRN2", target_bir_lowering=False, num_devices=1)
    arrays, aps = {}, {}
    given = {n: np.ascontiguousarray(v) for n, v in inputs.items()}
    given["shape_constants"] = shape_constants()
    for name, value in given.items():
        arrays[f"in_{name}"] = value
        aps[name] = nc.dram_tensor(f"in_{name}", value.shape, mybir.dt.from_np(value.dtype), kind="ExternalInput").ap()
    out = nc.dram_tensor("out", (1, T, D), F32, kind="ExternalOutput").ap()
    build(nc, aps, out)
    result = run_bass_kernel_spmd(nc, [arrays], core_ids=[0])
    return result.results[0]["out"]
```
